# Optimizing a Trainium2 kernel written in Bass

```python
import jax
import jax.numpy as jnp
from jax import lax
import numpy as np

D_MODEL = 1024
BATCH = 1
SEQ = 128
DEPTH = 2
DEC_BATCH = 1
DEC_SEQ = 512
PAST_LEN = 128

GRID_W = 64
N_EVEN = (DEPTH + 1) // 2
N_ODD = DEPTH // 2
RET_HEADS = 4
RET_DK = 64
RET_DV = 128
GDN_HEADS = 4
GDN_DK = 128
GDN_DV = 128
CONV_W = 3
CHUNK = 64
ATT_HEADS = 16
ATT_KV_HEADS = 4
ATT_HD = 64
ATT_GROUP = ATT_HEADS // ATT_KV_HEADS
Q_BLOCK = 128
ROPE_THETA = 10000.0
ROPE_PAIRS = ATT_HD // 4
FFN_HIDDEN = 2816
N_MOD = 9
EPS = 1e-6

RET_QK = RET_HEADS * RET_DK
RET_V = RET_HEADS * RET_DV
GDN_QK = GDN_HEADS * GDN_DK
GDN_V = GDN_HEADS * GDN_DV
EVEN_SPLITS = (RET_QK, RET_QK, RET_V, RET_V, GDN_QK, GDN_QK, GDN_V, GDN_V, 2 * GDN_HEADS, 2 * GDN_HEADS)
EVEN_IN = 2 * RET_QK + 2 * RET_V + 2 * GDN_QK + 2 * GDN_V + 4 * GDN_HEADS
EVEN_OUT = RET_V + GDN_V
ATT_Q = ATT_HEADS * ATT_HD
ATT_KV = ATT_KV_HEADS * ATT_HD
ODD_IN = ATT_Q + 2 * ATT_KV
ODD_OUT = ATT_Q

kernel_name = 'hybrid_prefix_dit_retention_gdn_gqa_step'

def _split(x, sizes):
    out, start = [], 0
    for s in sizes:
        out.append(x[..., start:start + s])
        start += s
    return out

def rmsnorm(x, w):
    xf = x.astype(jnp.float32)
    y = xf * lax.rsqrt(jnp.mean(xf * xf, axis=-1, keepdims=True) + EPS)
    return (y * w.astype(jnp.float32)).astype(x.dtype)

def l2norm(x):
    xf = x.astype(jnp.float32)
    return (xf * lax.rsqrt(jnp.sum(xf * xf, axis=-1, keepdims=True) + EPS)).astype(x.dtype)

def modulation(cond, w, b):
    m = jax.nn.silu(cond) @ w + b
    return m.reshape(cond.shape[0], N_MOD, D_MODEL)

def ada_norm(x, w, m, j):
    shift, scale = m[:, None, 3 * j], m[:, None, 3 * j + 1]
    return rmsnorm(x, w) * (1 + scale) + shift

def ffn_sublayer(x, m, j, w_norm, w_in, w_out):
    h = ada_norm(x, w_norm, m, j)
    a, b = _split(h @ w_in, (FFN_HIDDEN, FFN_HIDDEN))
    return x + 0.5 * m[:, None, 3 * j + 2] * ((jax.nn.silu(a) * b) @ w_out)

def _chunks(x):
    b, h, t = x.shape[:3]
    return x.reshape((b, h, t // CHUNK, CHUNK) + x.shape[3:])

def _decay_matrix(gc):
    causal = jnp.tril(jnp.ones((CHUNK, CHUNK), dtype=bool))
    diff = gc[..., :, None] - gc[..., None, :]
    return jnp.exp(jnp.where(causal, diff, -jnp.inf))

def chunk_decay_linear_attn(q, k, v, g, s0):
    out_dtype = q.dtype
    b, h, t, dv = v.shape
    qc, kc, vc = (_chunks(a.astype(jnp.float32)) for a in (q, k, v))
    gc = jnp.cumsum(_chunks(g.astype(jnp.float32)), axis=-1)
    decay = _decay_matrix(gc)
    scores = jnp.einsum('bhncd,bhnsd->bhncs', qc, kc) * decay
    o_intra = jnp.einsum('bhncs,bhnsv->bhncv', scores, vc)
    q_dec = qc * jnp.exp(gc)[..., None]
    k_dec = kc * jnp.exp(gc[..., -1:] - gc)[..., None]
    chunk_decay = jnp.exp(gc[..., -1])

    def step(state, xs):
        qd, kd, vv, cd = xs
        o = jnp.einsum('bhcd,bhdv->bhcv', qd, state)
        state = state * cd[..., None, None] + jnp.einsum('bhcd,bhcv->bhdv', kd, vv)
        return state, o

    xs = tuple(jnp.moveaxis(a, 2, 0) for a in (q_dec, k_dec, vc, chunk_decay))
    s_fin, o_inter = lax.scan(step, s0.astype(jnp.float32), xs)
    o = o_intra + jnp.moveaxis(o_inter, 0, 2)
    return o.reshape(b, h, t, dv).astype(out_dtype), s_fin

def chunk_gated_delta_rule(q, k, v, g, beta, s0):
    out_dtype = q.dtype
    b, h, t, dv = v.shape
    q, k, v = (a.astype(jnp.float32) for a in (q, k, v))
    beta = beta.astype(jnp.float32)[..., None]
    qc, kc = _chunks(q), _chunks(k)
    kbc, vbc = _chunks(k * beta), _chunks(v * beta)
    gc = jnp.cumsum(_chunks(g.astype(jnp.float32)), axis=-1)
    decay = _decay_matrix(gc)
    strict = jnp.tril(jnp.ones((CHUNK, CHUNK), dtype=bool), -1)
    m = jnp.where(strict, jnp.einsum('bhncd,bhnsd->bhncs', kbc, kc) * decay, 0.0)
    a_mat = m + jnp.eye(CHUNK, dtype=jnp.float32)
    rhs = jnp.concatenate([vbc, kbc * jnp.exp(gc)[..., None]], axis=-1)
    sol = lax.linalg.triangular_solve(a_mat, rhs, left_side=True, lower=True, unit_diagonal=True)
    u, w = sol[..., :dv], sol[..., dv:]
    attn = jnp.einsum('bhncd,bhnsd->bhncs', qc, kc) * decay
    q_dec = qc * jnp.exp(gc)[..., None]
    k_dec = kc * jnp.exp(gc[..., -1:] - gc)[..., None]
    chunk_decay = jnp.exp(gc[..., -1])

    def step(state, xs):
        qd, kd, uu, ww, at, cd = xs
        v_new = uu - jnp.einsum('bhcd,bhdv->bhcv', ww, state)
        o = jnp.einsum('bhcd,bhdv->bhcv', qd, state) + jnp.einsum('bhcs,bhsv->bhcv', at, v_new)
        state = state * cd[..., None, None] + jnp.einsum('bhcd,bhcv->bhdv', kd, v_new)
        return state, o

    xs = tuple(jnp.moveaxis(a, 2, 0) for a in (q_dec, k_dec, u, w, attn, chunk_decay))
    s_fin, o = lax.scan(step, s0.astype(jnp.float32), xs)
    o = jnp.moveaxis(o, 0, 2)
    return o.reshape(b, h, t, dv).astype(out_dtype), s_fin

def short_conv(x, w):
    return lax.conv_general_dilated(
        x, w[:, None, :].astype(x.dtype), window_strides=(1,),
        padding=[(CONV_W // 2, CONV_W // 2)], dimension_numbers=('NWC', 'WIO', 'NWC'),
        feature_group_count=x.shape[-1])

def even_mixer(h, w_in, w_out, decay_logit, ret_norm_w, conv_w, a_log, dt_bias, gdn_norm_w, s0_ret, s0_gdn):
    b, t, _ = h.shape
    rq, rk, rv, rg, gq, gk, gv, gg, ga, gb = _split(h @ w_in, EVEN_SPLITS)

    def heads(x, n):
        return x.reshape(b, t, n, -1).transpose(0, 2, 1, 3)

    def flip(x):
        return jnp.flip(x, axis=2)

    rq_h = heads(rq, RET_HEADS)
    rk_h = heads(rk, RET_HEADS) * RET_DK ** -0.5
    rv_h = heads(rv, RET_HEADS)
    log_gamma = jax.nn.log_sigmoid(decay_logit.astype(jnp.float32))
    g_f = jnp.broadcast_to(log_gamma[0][None, :, None], (b, RET_HEADS, t))
    g_b = jnp.broadcast_to(log_gamma[1][None, :, None], (b, RET_HEADS, t))
    o_f, sr_f = chunk_decay_linear_attn(rq_h, rk_h, rv_h, g_f, s0_ret[:, 0])
    o_b, sr_b = chunk_decay_linear_attn(flip(rq_h), flip(rk_h), flip(rv_h), g_b, s0_ret[:, 1])
    ret = rmsnorm(o_f + flip(o_b), ret_norm_w).transpose(0, 2, 1, 3).reshape(b, t, RET_V)
    ret = ret * jax.nn.silu(rg)

    qkv = jax.nn.silu(short_conv(jnp.concatenate([gq, gk, gv], axis=-1), conv_w))
    cq, ck, cv = _split(qkv, (GDN_QK, GDN_QK, GDN_V))
    q = l2norm(heads(cq, GDN_HEADS)) * GDN_DK ** -0.5
    k = l2norm(heads(ck, GDN_HEADS))
    v = heads(cv, GDN_HEADS)
    ga = ga.reshape(b, t, 2, GDN_HEADS).astype(jnp.float32)
    gb = gb.reshape(b, t, 2, GDN_HEADS).astype(jnp.float32)
    g = -jnp.exp(a_log.astype(jnp.float32)) * jax.nn.softplus(ga + dt_bias.astype(jnp.float32))
    g = g.transpose(2, 0, 3, 1)
    beta = jax.nn.sigmoid(gb).transpose(2, 0, 3, 1)
    od_f, sg_f = chunk_gated_delta_rule(q, k, v, g[0], beta[0], s0_gdn[:, 0])
    od_b, sg_b = chunk_gated_delta_rule(flip(q), flip(k), flip(v), jnp.flip(g[1], axis=-1),
                                        jnp.flip(beta[1], axis=-1), s0_gdn[:, 1])
    gdn = rmsnorm(od_f + flip(od_b), gdn_norm_w).transpose(0, 2, 1, 3).reshape(b, t, GDN_V)
    gdn = gdn * jax.nn.silu(gg)

    out = jnp.concatenate([ret, gdn], axis=-1) @ w_out
    return out, jnp.stack([sr_f, sr_b], axis=1), jnp.stack([sg_f, sg_b], axis=1)

def _rotate(x, ang):
    n = ang.shape[-1]
    cos = jnp.cos(ang)[None, :, None, :]
    sin = jnp.sin(ang)[None, :, None, :]
    xf = x.astype(jnp.float32)
    x1, x2 = xf[..., :n], xf[..., n:]
    return jnp.concatenate([x1 * cos - x2 * sin, x2 * cos + x1 * sin], axis=-1)

def axial_rope(x):
    t = x.shape[1]
    rows = t // GRID_W
    row = jnp.repeat(jnp.arange(rows, dtype=jnp.float32), GRID_W)
    col = (jnp.arange(rows * GRID_W) % GRID_W).astype(jnp.float32)
    inv = ROPE_THETA ** (-jnp.arange(ROPE_PAIRS, dtype=jnp.float32) / ROPE_PAIRS)
    half = ATT_HD // 2
    xr = _rotate(x[..., :half], row[:, None] * inv)
    xc = _rotate(x[..., half:], col[:, None] * inv)
    return jnp.concatenate([xr, xc], axis=-1).astype(x.dtype)

def block_attention(q, k, v):
    b, tq = q.shape[:2]
    nb = tq // Q_BLOCK
    qb = q.reshape(b, nb, Q_BLOCK, ATT_KV_HEADS, ATT_GROUP, ATT_HD).transpose(1, 0, 2, 3, 4, 5)
    scale = ATT_HD ** -0.5

    def one_block(qi):
        s = jnp.einsum('bqhgd,bkhd->bhgqk', qi, k, preferred_element_type=jnp.float32) * scale
        p = jax.nn.softmax(s, axis=-1).astype(v.dtype)
        return jnp.einsum('bhgqk,bkhd->bqhgd', p, v)

    o = lax.map(one_block, qb)
    return o.transpose(1, 0, 2, 3, 4, 5).reshape(b, tq, ATT_HEADS * ATT_HD)

def odd_mixer(h, w_in, w_out, q_norm_w, k_norm_w, ctx_k=None, ctx_v=None):
    b, t, _ = h.shape
    q, k, v = _split(h @ w_in, (ATT_Q, ATT_KV, ATT_KV))
    q = rmsnorm(q.reshape(b, t, ATT_HEADS, ATT_HD), q_norm_w)
    k = rmsnorm(k.reshape(b, t, ATT_KV_HEADS, ATT_HD), k_norm_w)
    v = v.reshape(b, t, ATT_KV_HEADS, ATT_HD)
    if ctx_k is None:
        o = block_attention(q, k, v)
    else:
        q, k = axial_rope(q), axial_rope(k)
        o = block_attention(q, jnp.concatenate([ctx_k, k], axis=1), jnp.concatenate([ctx_v, v], axis=1))
    return o @ w_out, k, v

def setup_inputs(seed: int = 0) -> dict:
    key = jax.random.key(seed)
    ks = jax.random.split(key, 26)
    f32 = jnp.float32

    def nrm(k, shape, s):
        return jax.random.normal(k, shape, f32) * s

    gamma = 1.0 - 2.0 ** (-5.0 - jnp.arange(RET_HEADS, dtype=f32))
    dt = jnp.exp(jax.random.uniform(ks[19], (N_EVEN, 2, GDN_HEADS), f32, np.log(1e-3), np.log(1e-1)))
    return {
        'x_prompt': nrm(ks[0], (BATCH, SEQ, D_MODEL), 1.0),
        'x_sample': nrm(ks[1], (DEC_BATCH, DEC_SEQ, D_MODEL), 1.0),
        'state_ret': nrm(ks[2], (DEC_BATCH, N_EVEN, 2, RET_HEADS, RET_DK, RET_DV), 0.5),
        'state_gdn': nrm(ks[3], (DEC_BATCH, N_EVEN, 2, GDN_HEADS, GDN_DK, GDN_DV), 0.5),
        'cache_k': nrm(ks[4], (DEC_BATCH, N_ODD, PAST_LEN, ATT_KV_HEADS, ATT_HD), 1.0),
        'cache_v': nrm(ks[5], (DEC_BATCH, N_ODD, PAST_LEN, ATT_KV_HEADS, ATT_HD), 1.0),
        'c': nrm(ks[6], (DEC_BATCH, D_MODEL), 1.0),
        'c_ctx': nrm(ks[7], (D_MODEL,), 1.0),
        'mod_w': nrm(ks[8], (DEPTH, D_MODEL, N_MOD * D_MODEL), 0.02),
        'mod_b': nrm(ks[9], (DEPTH, N_MOD * D_MODEL), 0.02),
        'norm_w': 1.0 + nrm(ks[10], (DEPTH, 3, D_MODEL), 0.02),
        'ffn_w_in': nrm(ks[11], (DEPTH, 2, D_MODEL, 2 * FFN_HIDDEN), D_MODEL ** -0.5),
        'ffn_w_out': nrm(ks[12], (DEPTH, 2, FFN_HIDDEN, D_MODEL), FFN_HIDDEN ** -0.5),
        'even_w_in': nrm(ks[13], (N_EVEN, D_MODEL, EVEN_IN), D_MODEL ** -0.5),
        'even_w_out': nrm(ks[14], (N_EVEN, EVEN_OUT, D_MODEL), EVEN_OUT ** -0.5),
        'ret_decay_logit': jnp.log(gamma / (1.0 - gamma)) + nrm(ks[15], (N_EVEN, 2, RET_HEADS), 0.1),
        'ret_norm_w': 1.0 + nrm(ks[16], (N_EVEN, RET_DV), 0.02),
        'gdn_conv_w': nrm(ks[17], (N_EVEN, CONV_W, 2 * GDN_QK + GDN_V), CONV_W ** -0.5),
        'gdn_A_log': jnp.log(jax.random.uniform(ks[18], (N_EVEN, 2, GDN_HEADS), f32, 1.0, 16.0)),
        'gdn_dt_bias': dt + jnp.log(-jnp.expm1(-dt)),
        'gdn_norm_w': 1.0 + nrm(ks[20], (N_EVEN, GDN_DV), 0.02),
        'odd_w_in': nrm(ks[21], (N_ODD, D_MODEL, ODD_IN), D_MODEL ** -0.5),
        'odd_w_out': nrm(ks[22], (N_ODD, ODD_OUT, D_MODEL), ODD_OUT ** -0.5),
        'q_norm_w': 1.0 + nrm(ks[23], (N_ODD, ATT_HD), 0.02),
        'k_norm_w': 1.0 + nrm(ks[24], (N_ODD, ATT_HD), 0.02),
        'final_norm_w': 1.0 + nrm(ks[25], (D_MODEL,), 0.02),
    }

def reference(x_prompt, x_sample, state_ret, state_gdn, cache_k, cache_v, c, c_ctx,
              mod_w, mod_b, norm_w, ffn_w_in, ffn_w_out, even_w_in, even_w_out,
              ret_decay_logit, ret_norm_w, gdn_conv_w, gdn_A_log, gdn_dt_bias, gdn_norm_w,
              odd_w_in, odd_w_out, q_norm_w, k_norm_w, final_norm_w):
    xp, xs = x_prompt, x_sample
    bp = xp.shape[0]
    zero_ret = jnp.zeros((bp, 2, RET_HEADS, RET_DK, RET_DV), jnp.float32)
    zero_gdn = jnp.zeros((bp, 2, GDN_HEADS, GDN_DK, GDN_DV), jnp.float32)
    new_ret, new_gdn, new_k, new_v = [], [], [], []
    for l in range(DEPTH):
        mp = modulation(c_ctx[None], mod_w[l], mod_b[l])
        ms = modulation(c, mod_w[l], mod_b[l])
        xp = ffn_sublayer(xp, mp, 0, norm_w[l, 0], ffn_w_in[l, 0], ffn_w_out[l, 0])
        xs = ffn_sublayer(xs, ms, 0, norm_w[l, 0], ffn_w_in[l, 0], ffn_w_out[l, 0])
        hp = ada_norm(xp, norm_w[l, 1], mp, 1)
        hs = ada_norm(xs, norm_w[l, 1], ms, 1)
        if l % 2 == 0:
            e = l // 2
            prm = (even_w_in[e], even_w_out[e], ret_decay_logit[e], ret_norm_w[e], gdn_conv_w[e],
                   gdn_A_log[e], gdn_dt_bias[e], gdn_norm_w[e])
            op, sr, sg = even_mixer(hp, *prm, zero_ret, zero_gdn)
            os_, _, _ = even_mixer(hs, *prm, state_ret[:, e], state_gdn[:, e])
            new_ret.append(sr)
            new_gdn.append(sg)
        else:
            o = l // 2
            prm = (odd_w_in[o], odd_w_out[o], q_norm_w[o], k_norm_w[o])
            op, kp, vp = odd_mixer(hp, *prm)
            os_, _, _ = odd_mixer(hs, *prm, cache_k[:, o], cache_v[:, o])
            new_k.append(kp)
            new_v.append(vp)
        xp = xp + mp[:, None, 5] * op
        xs = xs + ms[:, None, 5] * os_
        xp = ffn_sublayer(xp, mp, 2, norm_w[l, 2], ffn_w_in[l, 1], ffn_w_out[l, 1])
        xs = ffn_sublayer(xs, ms, 2, norm_w[l, 2], ffn_w_in[l, 1], ffn_w_out[l, 1])
    y_prompt = rmsnorm(xp, final_norm_w)
    y_sample = rmsnorm(xs, final_norm_w)
    new_state_ret = jnp.stack(new_ret, axis=1)
    new_state_gdn = jnp.stack(new_gdn, axis=1)
    new_cache_k = jnp.stack(new_k, axis=1)
    new_cache_v = jnp.stack(new_v, axis=1)
    return (y_prompt, y_sample, new_state_ret, new_state_gdn, new_cache_k, new_cache_v)


_drawn_inputs = setup_inputs


def setup_inputs(seed=0):
    import zlib

    import numpy as np

    out = dict(_drawn_inputs(seed))
    spreads = {}
    factors = {'state_ret': 2.825,
     'cache_k': 6.278,
     'cache_v': 4.999,
     'ret_norm_w': 8.0,
     'gdn_norm_w': 8.0,
     'q_norm_w': 8.0,
     'final_norm_w': 2.8}
    for name, (base, spread) in spreads.items():
        noise = np.random.default_rng([zlib.crc32(name.encode()), seed]).standard_normal(out[name].shape)
        drawn = base * np.exp(spread * noise) if base else spread * noise
        out[name] = jnp.asarray(drawn.astype(out[name].dtype))
    for name, factor in factors.items():
        out[name] = (out[name] * factor).astype(out[name].dtype)
    return out
```

```python
import concourse.bass as bass
from concourse import mybir
from contextlib import ExitStack

F32 = mybir.dt.float32
F32R = mybir.dt.float32r
BF16 = mybir.dt.bfloat16
ALU = mybir.AluOpType
ACT = mybir.ActivationFunctionType
AX = mybir.AxisListType
ds = bass.ds

P = 128
D = 1024
DT = D // P
NCTX, NLAT = 128, 512
T = NCTX + NLAT
TT = T // P
HALF = T // 2
FH = 2816
NMOD = 9
MT = NMOD * DT
EPS = 1e-6
KT = 8
SLAB = 256
FFN_CHUNKS = (8, 8, 6)
assert sum(FFN_CHUNKS) * P == FH
MS = 512
MSLABS = NMOD * D // MS
RH, RDK, RDV = 4, 64, 128
GH, GDK = 4, 128
EVEN_TILES = 28
RQ0, RK0, RV0, RG0, GQ0, GK0, GV0, GG0 = 0, 2, 4, 8, 12, 16, 20, 24
AH, KVH, HD = 16, 4, 64
ROWS = dict(norm=0, final=48, cond=56, conv=72)
NROWS = 108
LEVELS = (1, 2, 4, 8, 16, 32, 64)
STRIP = 896

G_FFN = sum(FFN_CHUNKS) + 3 * 4
GROUPS = {}
_g = 0
for _name, _n in (("ffn00", G_FFN), ("even_in", 14), ("even_out", 4), ("ffn01", G_FFN),
                  ("ffn10", G_FFN), ("odd_in", 6), ("odd_out", 4), ("ffn11", G_FFN)):
    GROUPS[_name] = _g
    _g += _n
NGROUPS = _g
MOD_FIRST = 4
MOD_PLAN = {"ffn00": {0: (4, 0, 4), 1: (8, 0, 8), 2: (10, 0, 10), 3: (14, 0, 14), 4: (16, 1, 0), 5: (19, 0, 16)},
            "ffn01": {0: (21, 1, 3), 1: (25, 1, 7), 2: (27, 1, 9), 3: (31, 1, 13), 4: (33, 1, 15)}}
MOD_ALL = 2 * MSLABS
MOD_ORDER = {q: (0, q) for q in range(MOD_FIRST)}
for _name, _loops in MOD_PLAN.items():
    for _n, (_q, _layer, _m) in _loops.items():
        _chunk = FFN_CHUNKS[_n // 2]
        for _i in range(_chunk // 2 if _n % 2 == 0 else 2):
            MOD_ORDER[_q + _i] = (_layer, _m + _i)
assert sorted(MOD_ORDER) == list(range(MOD_ALL)) and len(set(MOD_ORDER.values())) == MOD_ALL


def bass_hybrid_step(nc, ins, outs):
    with ExitStack() as ctx:
        base = [(nc.sbuf_base + 63) // 64 * 64]
        top = 229344

        def sem(name):
            return ctx.enter_context(nc.semaphore(name))

        def at(name, shape, offset, dt=F32):
            size = 2 if dt == BF16 else 4
            for n in shape[1:]:
                size *= n
            assert offset + size <= top, (name, offset + size)
            return nc.alloc_sbuf_tensor_at(name, shape, dt, offset=offset)

        def take(nbytes):
            o = base[0]
            base[0] += (nbytes + 63) // 64 * 64
            assert base[0] <= top, base[0]
            return o

        TILE = T * 4
        o_x, o_h, o_w, o_u, o_t = take(DT * TILE), take(2 * DT * TILE), take(6 * KT * SLAB * 4), \
            take(EVEN_TILES * TILE), take(4 * TILE)
        o_c = base[0]
        x = at("x", [P, DT, T], o_x)
        h_hi = at("h_hi", [P, DT, T], o_h, F32R)
        h_lo = at("h_lo", [P, DT, T], o_h + DT * TILE, F32R)
        WB = KT * SLAB * 4
        w_raw = [at(f"w_raw{s}", [P, KT, SLAB], o_w + s * WB) for s in range(2)]
        w_hi = [at(f"w_hi{s}", [P, KT, SLAB], o_w + (2 + s) * WB, F32R) for s in range(2)]
        w_lo = [at(f"w_lo{s}", [P, KT, SLAB], o_w + (4 + s) * WB, F32R) for s in range(2)]
        hid_hi = at("hid_hi", [P, KT, T], o_u, F32R)
        hid_lo = at("hid_lo", [P, KT, T], o_u + KT * TILE, F32R)
        mod_raw = [at(f"mod_raw{k}", [P, 4, MS], o_u + 2 * KT * TILE + k * 4 * MS * 4) for k in range(2)]
        proj = at("proj", [P, EVEN_TILES, T], o_u)
        tmp_a = [at(f"tmp_a{s}", [P, T], o_t + s * TILE) for s in range(2)]
        tmp_b = [at(f"tmp_b{s}", [P, T], o_t + (2 + s) * TILE) for s in range(2)]
        sq = at("sq", [P, 2, T], o_t)
        sq_acc = tmp_b[0]
        x_tok = at("x_tok", [P, TT, D], o_h)
        lvl_st = at("lvl_st", [P, 2, len(LEVELS), P], o_u)
        rows = at("rows", [P, 3, P], o_t)

        def const(name, shape, dt=F32):
            size = 2 if dt == BF16 else 4
            for n in shape[1:]:
                size *= n
            return at(name, shape, take(size), dt)

        mod_acc = const("mod_acc", [P, 2, MS])
        ident = const("ident", [P, P])
        tri = const("tri", [P, 2, P])
        lvl = const("lvl", [P, 2, len(LEVELS), P], BF16)
        ones = const("ones", [P, P])
        eps = const("eps", [P, 1])
        mods = const("mods", [P, 2 * MT, 2])
        mod_b = const("mod_b", [P, 2 * MT])
        vecs = const("vecs", [P, NROWS])
        cond = const("cond", [P, 2, DT])
        ada_scale = const("ada_scale", [P, DT, 2])
        gate = const("gate", [P, DT, 2])
        stat_sd = const("stat_sd", [P, 100])
        stat_r = const("stat_r", [P, 100])

        ps = ctx.enter_context(nc.psum_tensor("ps", [P, 8, 512], F32))
        psf = ps[:, :, :].rearrange("p b n -> p (b n)")

        consts_in, rows_in, x_in = sem("consts_in"), sem("rows_in"), sem("x_in")
        consts_set = sem("consts_set")
        lvl_in, lvl_ready = sem("lvl_in"), sem("lvl_ready")
        rows_mm, vecs_ready, cond_ready = sem("rows_mm"), sem("vecs_ready"), sem("cond_ready")
        x_mm, x_act, x_dve = sem("x_mm"), sem("x_act"), sem("x_dve")
        w_in = [sem(f"w_in{s}") for s in range(2)]
        whi_ready, wlo_ready = sem("whi_ready"), sem("wlo_ready")
        group_mm, group_out = sem("group_mm"), sem("group_out")
        silu_done, hid_hi_ready, hid_lo_ready = sem("silu_done"), sem("hid_hi_ready"), sem("hid_lo_ready")
        mod_in = [sem(f"mod_in{k}") for k in range(2)]
        mod_step, mod_mm, mod_ready = sem("mod_step"), sem("mod_mm"), sem("mod_ready")
        gate_ready, ada_step, ada_ready = sem("gate_ready"), sem("ada_step"), sem("ada_ready")
        sq_ready, sq_mm, sd_ready, r_ready, r_mm = sem("sq_ready"), sem("sq_mm"), sem("sd_ready"), sem("r_ready"), sem("r_mm")
        xr_ready, sq_sum, hhi_ready, hlo_ready = sem("xr_ready"), sem("sq_sum"), sem("hhi_ready"), sem("hlo_ready")
        y_mm, y_out, out_done = sem("y_mm"), sem("y_out"), sem("out_done")

        LOOPS = []
        g = 0
        for c, n in enumerate(FFN_CHUNKS):
            LOOPS.append(("up", c, g, n // 2))
            LOOPS.append(("down", c, g + n, 2))
            g += n + 4
        FFNS = ("ffn00", "ffn01", "ffn10", "ffn11")
        NORM_AFTER = {"ffn00": 1, "even_out": 2, "ffn01": 3, "ffn10": 4, "odd_out": 5, "ffn11": 6}

        def ffn_at(name):
            f = FFNS.index(name)
            return f // 2, f % 2, f

        def sp_slab_free(sp, g):
            if isinstance(g, int) and g < 2:
                return
            sp.wait_ge(wlo_ready, g - 1)

        def sp_ffn(sp, name):
            l, f, _ = ffn_at(name)
            w1 = ins["ffn_w_in"][l, f].rearrange("(k p) n -> p k n", p=P)
            w2 = ins["ffn_w_out"][l, f].rearrange("(k p) n -> p k n", p=P)
            mw = [ins["mod_w"][i].rearrange("(k p) n -> p k n", p=P) for i in range(2)]
            for n, (kind, c, g0, bodies) in enumerate(LOOPS):
                g0 += GROUPS[name]
                k0, kn = sum(FFN_CHUNKS[:c]), FFN_CHUNKS[c]
                plan = MOD_PLAN.get(name, {}).get(n)

                def body(i):
                    for s in range(2):
                        sp_slab_free(sp, g0 + 2 * i + s)
                        if kind == "up":
                            col = (k0 + s) * P + 2 * P * i
                            parts = ((w_raw[s][:, :, 0:P], w1[:, :, ds(col, P)]),
                                     (w_raw[s][:, :, P:SLAB], w1[:, :, ds(FH + col, P)]))
                        else:
                            col = 2 * SLAB * i + s * SLAB
                            m = kn // 2
                            parts = ((w_raw[s][:, 0:m, :], w2[:, k0:k0 + m, ds(col, SLAB)]),
                                     (w_raw[s][:, m:kn, :], w2[:, k0 + m:k0 + kn, ds(col, SLAB)]))
                        for dst, src in parts:
                            sp.dma_start(dst, src).then_inc(w_in[s], 16)
                        if plan and s == 0:
                            sp_mod_half(sp, 1, plan[0] + i, mw[plan[1]], plan[2] + i)
                        if plan and s == 1 and not isinstance(i, int):
                            sp_mod_half(sp, 0, plan[0] + i + 1, mw[plan[1]], plan[2] + i + 1)
                        if plan and s == 1 and isinstance(i, int):
                            q = plan[0] + i + 1
                            if q < MOD_ALL:
                                sp_mod_half(sp, 0, q, mw[MOD_ORDER[q][0]], MOD_ORDER[q][1])

                body_loop(sp, g0, bodies, body, peel=bool(plan))

        def sp_linear(sp, name, w, groups):
            w = w.rearrange("(k p) n -> p k n", p=P)
            g0 = GROUPS[name]

            def body(i):
                for s in range(2):
                    sp_slab_free(sp, g0 + 2 * i + s)
                    for m in range(2):
                        sp.dma_start(w_raw[s][:, 4 * m:4 * m + 4, :],
                                     w[:, 4 * m:4 * m + 4, ds(2 * SLAB * i + s * SLAB, SLAB)]).then_inc(w_in[s], 16)

            body_loop(sp, g0, groups // 2, body)

        def sp_mod_half(sp, k, q, mw, m):
            if not (isinstance(q, int) and q == 0):
                sp.wait_ge(mod_step, 16 * (q - 1) + 8 * (k + 1))
            sp.dma_start(mod_raw[k][:, :, :], mw[:, 4 * k:4 * k + 4, ds(m * MS, MS)]).then_inc(mod_in[k], 16)

        def body_loop(eng, g0, bodies, body, peel=False):
            first, last = int(g0 == 0), bodies - int(g0 + 2 * bodies == NGROUPS or peel)
            if first:
                body(0)
            if last > first:
                with eng.Fori(first, last) as i:
                    body(i)
            if last < bodies:
                body(bodies - 1)

        def act_split(act, g, s):
            if isinstance(g, int) and g >= NGROUPS:
                return
            act.wait_ge(w_in[s], slab_uses(g, s))
            if not isinstance(g, int) or g >= 2:
                act.wait_ge(group_mm, g - 1)
            nc.scalar.copy(w_hi[s][:, :, :], w_raw[s][:, :, :]).then_inc(whi_ready, 1)

        def dve_split(dve, g, s):
            if isinstance(g, int) and g >= NGROUPS:
                return
            dve.wait_ge(whi_ready, g + 1)
            nc.vector.tensor_tensor(w_lo[s][:, :, :], w_raw[s][:, :, :], w_hi[s][:, :, :].bitcast(F32),
                                    ALU.subtract).then_inc(wlo_ready, 1)

        def slab_uses(g, s):
            return 16 * (g - s) + 32

        def pe_group(pe, g, s, kn, hi, lo, ready=None, mod=None, after_mod=None):
            pe.wait_ge(wlo_ready, g + 1)
            if not isinstance(g, int) or g >= 2:
                pe.wait_ge(group_out, g - 1)
            if after_mod is not None:
                pe.wait_ge(mod_ready, after_mod + 1)
            for k in range(kn):
                if ready:
                    pe.wait_ge(ready[0], ready[1] + k + 1)
                if mod is not None and k == kn - 1:
                    if not isinstance(g, int) or g >= 1:
                        pe.wait_ge(group_out, g)
                    pe_mod(pe, mod)
                for n in range(2):
                    cols = slice(n * P, n * P + P)
                    for w, v, first, last in ((w_hi, hi, True, False), (w_hi, lo, False, False), (w_lo, hi, False, True)):
                        for b in range(2):
                            mm = nc.tensor.matmul(ps[:, 4 * s + 2 * n + b, 0:HALF], w[s][:, k, cols],
                                                  v[:, k, b * HALF:(b + 1) * HALF],
                                                  start=(first and k == 0), stop=(last and k == kn - 1))
            mm.then_inc(group_mm, 1)

        def dve_mod_half(dve, k, q):
            dve.wait_ge(mod_in[k], 16 * (q + 1))
            if k == 0 and not (isinstance(q, int) and q == 0):
                dve.wait_ge(mod_mm, q)
            for j in range(4):
                kt = 4 * k + j
                for s in range(2):
                    if kt == 0:
                        nc.vector.tensor_scalar(mod_acc[:, s, :], mod_raw[k][:, j, :], cond[:, s, kt:kt + 1], None,
                                                ALU.mult).then_inc(mod_step, 1)
                    else:
                        dve.wait_ge(mod_step, 16 * q + 2 * (kt - 1) + s + 1)
                        nc.vector.scalar_tensor_tensor(mod_acc[:, s, :], mod_raw[k][:, j, :], cond[:, s, kt:kt + 1],
                                                       mod_acc[:, s, :], ALU.mult, ALU.add).then_inc(mod_step, 1)

        def pe_mod(pe, q):
            pe.wait_ge(mod_step, 16 * (q + 1))
            for n in range(MS // P):
                for s in range(2):
                    mm = nc.tensor.matmul(ps[:, 7, HALF + 2 * n + s:HALF + 2 * n + s + 1],
                                          mod_acc[:, s, n * P:(n + 1) * P], ones[:, 0:1], start=True, stop=True)
            mm.then_inc(mod_mm, 1)

        def dve_mod_out(dve, q, layer, m):
            dve.wait_ge(mod_mm, q + 1)
            t = layer * MT + m * (MS // P)
            src = ps[:, 7, HALF:HALF + 8].rearrange("p (n s) -> p n s", s=2)
            nc.vector.tensor_tensor(mods[:, ds(t, 4), :], src, mod_b[:, ds(t, 4)].unsqueeze(2).to_broadcast([P, 4, 2]),
                                    ALU.add).then_inc(mod_ready, 1)

        R_BANK = 6
        STREAMS = ((0, 0, NCTX), (1, NCTX, T))
        PIECES = ((0, 0, 0, NCTX), (1, 0, NCTX, HALF), (1, 1, 0, HALF))

        TMP = tmp_a + tmp_b

        def act_squares(act, a, g, q):
            if g is not None:
                act.wait_ge(group_out, g + 1)
            act.wait_ge(sq_sum, 9 * a + 2 * q + 1)
            nc.scalar.activation(sq[:, :, :], x[:, ds(2 * q, 2), :], ACT.Square).then_inc(sq_ready, 1)

        def sums_cleared(eng, engine, a):
            if a:
                eng.wait_ge(sq_mm, a)
            engine.memset(sq_acc[:, :], 0.0).then_inc(sq_sum, 1)

        def add_squares(eng, engine, a, q):
            eng.wait_ge(sq_ready, 4 * a + q + 1)
            for n in range(2):
                eng.wait_ge(sq_sum, 9 * a + 2 * q + n + 1)
                engine.tensor_tensor(sq_acc[:, :], sq_acc[:, :], sq[:, n, :], ALU.add).then_inc(sq_sum, 1)

        def act_ada(act, a, layer, j):
            act.wait_ge(sq_mm, a + 1)
            nc.scalar.activation(stat_sd[:, 0:TT], ps[:, 0, 0:TT], ACT.Sqrt, bias=eps[:, :],
                                 scale=1.0 / D).then_inc(sd_ready, 1)
            for t in range(DT if j is not None else 0):
                act.wait_ge(xr_ready, DT * a + t + 1)
                for s, c0, c1 in STREAMS:
                    ins_ = nc.scalar.activation(h_hi[:, t, c0:c1], TMP[t % 4][:, c0:c1], ACT.Identity,
                                                bias=mods[:, layer * MT + 3 * j * DT + t, s:s + 1])
                ins_.then_inc(hhi_ready, 1)

        def pe_ada(pe, a):
            pe.wait_ge(sq_sum, 9 * (a + 1))
            for b in range(TT):
                mm = nc.tensor.matmul(ps[:, 0, b:b + 1], sq_acc[:, b * P:(b + 1) * P], ones[:, 0:1],
                                      start=True, stop=True)
            mm.then_inc(sq_mm, 1)
            pe.wait_ge(r_ready, a + 1)
            for b in range(TT):
                o = R_BANK * 512 + b * P
                mm = nc.tensor.matmul(psf[:, o:o + P], stat_r[:, b:b + 1].to_broadcast([P, P]), ident[:, :],
                                      start=True, stop=True)
            mm.then_inc(r_mm, 1)

        def dve_ada(dve, a, layer, j, mod_count):
            if j is not None:
                dve.wait_ge(mod_ready, mod_count)
                t0 = layer * MT + (3 * j + 1) * DT
                w0 = ROWS["norm"] + (layer * 3 + j) * DT
                wn = vecs[:, w0:w0 + DT].unsqueeze(2).to_broadcast([P, DT, 2])
                nc.vector.tensor_scalar(ada_scale[:, :, :], mods[:, t0:t0 + DT, :], 1.0, None,
                                        ALU.add).then_inc(ada_step, 1)
                dve.wait_ge(ada_step, a + 1)
                nc.vector.tensor_tensor(ada_scale[:, :, :], ada_scale[:, :, :], wn, ALU.mult).then_inc(ada_ready, 1)
            dve.wait_ge(sd_ready, a + 1)
            nc.vector.reciprocal(stat_r[:, 0:TT], stat_sd[:, 0:TT]).then_inc(r_ready, 1)
            dve.wait_ge(r_mm, a + 1)
            if j is not None:
                dve.wait_ge(ada_ready, a + 1)

            def scaled(t):
                for s, c0, c1 in STREAMS:
                    v = nc.vector.scalar_tensor_tensor(TMP[t % 4][:, c0:c1], x[:, t, c0:c1], ada_scale[:, t, s:s + 1],
                                                       psf[:, R_BANK * 512 + c0:R_BANK * 512 + c1], ALU.mult, ALU.mult)
                v.then_inc(xr_ready, 1)

            if j is None:
                for t in range(DT):
                    if t >= 4:
                        dve.wait_ge(y_mm, t - 3)
                    nc.vector.scalar_tensor_tensor(TMP[t % 4][:, :], x[:, t, :], vecs[:, ROWS["final"] + t:ROWS["final"] + t + 1],
                                                   psf[:, R_BANK * 512:R_BANK * 512 + T], ALU.mult, ALU.mult).then_inc(hlo_ready, 1)
                return
            scaled(0)
            for t in range(DT):
                if t + 1 < DT:
                    scaled(t + 1)
                dve.wait_ge(hhi_ready, DT * a + t + 1)
                for s, c0, c1 in STREAMS:
                    v = nc.vector.scalar_tensor_tensor(h_lo[:, t, c0:c1], TMP[t % 4][:, c0:c1],
                                                       mods[:, layer * MT + 3 * j * DT + t, s:s + 1],
                                                       h_hi[:, t, c0:c1].bitcast(F32), ALU.add, ALU.subtract)
                v.then_inc(hlo_ready, 1)

        def act_ffn(act, name):
            f = FFNS.index(name)
            for n, (kind, c, g0, bodies) in enumerate(LOOPS):
                g0 += GROUPS[name]
                up0 = f * sum(FFN_CHUNKS) + sum(FFN_CHUNKS[:c])

                def body(i):
                    for s in range(2):
                        g = g0 + 2 * i + s
                        act.wait_ge(group_mm, g + 1)
                        if kind == "up":
                            if not isinstance(g, int) or g >= 2:
                                act.wait_ge(group_out, g - 1)
                            nc.scalar.activation(tmp_a[s][:, :].rearrange("p (b n) -> p b n", b=2),
                                                 ps[:, 4 * s:4 * s + 2, 0:HALF], ACT.Silu).then_inc(silu_done, 1)
                        if n == len(LOOPS) - 1:
                            act_squares(act, NORM_AFTER[name], g, 2 * i + s)
                        act_split(act, g + 2, s)
                        if kind == "up":
                            act.wait_ge(group_out, g + 1)
                            nc.scalar.copy(hid_hi[:, ds(2 * i + s, 1), :],
                                           tmp_b[s][:, :].unsqueeze(1)).then_inc(hid_hi_ready, 1)

                body_loop(act, g0, bodies, body)

        def dve_gate(dve, k, layer, j, factor, mod_count):
            dve.wait_ge(mod_ready, mod_count)
            if k:
                dve.wait_ge(group_out, GATE_FREE[k])
            t0 = layer * MT + (3 * j + 2) * DT
            nc.vector.tensor_scalar(gate[:, :, :], mods[:, t0:t0 + DT, :], factor, None, ALU.mult).then_inc(gate_ready, 1)

        def dve_add_group(dve, g, s, tile, k):
            dve.wait_ge(group_mm, g + 1)
            dve.wait_ge(gate_ready, k + 1)
            dve.wait_ge(group_out, g)
            for n in range(2):
                for st, b, c0, c1 in PIECES:
                    o = b * HALF + c0
                    v = x[:, ds(tile + n, 1), o:o + c1 - c0]
                    last = nc.vector.scalar_tensor_tensor(v, ps[:, 4 * s + 2 * n + b:4 * s + 2 * n + b + 1, c0:c1],
                                                          gate[:, ds(tile + n, 1), st:st + 1], v, ALU.mult, ALU.add)
            last.then_inc(group_out, 1)

        def dve_ffn(dve, name, k, mod_count):
            f = FFNS.index(name)
            for n, (kind, c, g0, bodies) in enumerate(LOOPS):
                g0 += GROUPS[name]
                up0 = f * sum(FFN_CHUNKS) + sum(FFN_CHUNKS[:c])
                plan = MOD_PLAN.get(name, {}).get(n)
                if n == 1:
                    dve_gate(dve, k, f // 2, 2 * (f % 2), 0.5, mod_count)
                if n == len(LOOPS) - 1:
                    sums_cleared(dve, nc.vector, NORM_AFTER[name])

                def body(i):
                    for s in range(2):
                        g = g0 + 2 * i + s
                        fi = up0 + 2 * i + s
                        if plan and s == 0:
                            dve_mod_half(dve, 1, plan[0] + i)
                            dve_mod_out(dve, plan[0] + i, plan[1], plan[2] + i)
                        if plan and s == 1 and not (isinstance(i, int) and plan[0] + i + 1 == MOD_ALL):
                            dve_mod_half(dve, 0, plan[0] + i + 1)
                        if kind == "up":
                            dve.wait_ge(silu_done, fi + 1)
                            if not isinstance(fi, int) or fi >= 2:
                                dve.wait_ge(hid_lo_ready, fi - 1)
                            nc.vector.tensor_tensor(tmp_b[s][:, :].rearrange("p (b n) -> p b n", b=2),
                                                    tmp_a[s][:, :].rearrange("p (b n) -> p b n", b=2),
                                                    ps[:, 4 * s + 2:4 * s + 4, 0:HALF], ALU.mult).then_inc(group_out, 1)
                        else:
                            dve_add_group(dve, g, s, 4 * i + 2 * s, k)
                        if n == len(LOOPS) - 1:
                            add_squares(dve, nc.vector, NORM_AFTER[name], 2 * i + s)
                        dve_split(dve, g + 2, s)
                        if kind == "up":
                            dve.wait_ge(hid_hi_ready, fi + 1)
                            nc.vector.tensor_tensor(hid_lo[:, ds(2 * i + s, 1), :], tmp_b[s][:, :].unsqueeze(1),
                                                    hid_hi[:, ds(2 * i + s, 1), :].bitcast(F32),
                                                    ALU.subtract).then_inc(hid_lo_ready, 1)

                body_loop(dve, g0, bodies, body, peel=bool(plan) and plan[0] + bodies == MOD_ALL)

        def pe_ffn(pe, name, a):
            f = FFNS.index(name)
            for n, (kind, c, g0, bodies) in enumerate(LOOPS):
                g0 += GROUPS[name]
                up0 = f * sum(FFN_CHUNKS) + sum(FFN_CHUNKS[:c])
                plan = MOD_PLAN.get(name, {}).get(n)

                def body(i):
                    for s in range(2):
                        g = g0 + 2 * i + s
                        if kind == "up":
                            v = (KT, h_hi, h_lo, (hlo_ready, DT * a))
                        else:
                            v = (FFN_CHUNKS[c], hid_hi, hid_lo, (hid_lo_ready, up0))
                        pe_group(pe, g, s, *v, mod=plan[0] + i if plan and s == 0 else None,
                                 after_mod=plan[0] + i if plan and s == 1 else None)

                body_loop(pe, g0, bodies, body)


        def act_linear(act, name, groups):
            def body(i):
                for s in range(2):
                    if name in NORM_AFTER:
                        act_squares(act, NORM_AFTER[name], GROUPS[name] + 2 * i + s, 2 * i + s)
                    act_split(act, GROUPS[name] + 2 * i + s + 2, s)

            body_loop(act, GROUPS[name], groups // 2, body)

        def pe_linear(pe, name, groups, ready):
            def body(i):
                for s in range(2):
                    pe_group(pe, GROUPS[name] + 2 * i + s, s, KT, h_hi, h_lo, ready)

            body_loop(pe, GROUPS[name], groups // 2, body)

        def dve_add_groups(dve, name, groups, k):
            def body(i):
                for s in range(2):
                    dve_add_group(dve, GROUPS[name] + 2 * i + s, s, 4 * i + 2 * s, k)
                    add_squares(dve, nc.vector, NORM_AFTER[name], 2 * i + s)
                    dve_split(dve, GROUPS[name] + 2 * i + s + 2, s)

            sums_cleared(dve, nc.vector, NORM_AFTER[name])
            body_loop(dve, GROUPS[name], groups // 2, body)

        def dve_take_group(dve, g, s, tile):
            dve.wait_ge(group_mm, g + 1)
            nc.vector.tensor_copy(proj[:, ds(tile, 2), :].rearrange("p t (b n) -> p (t b) n", b=2),
                                  ps[:, 4 * s:4 * s + 4, 0:HALF]).then_inc(group_out, 1)

        tn_sq, tn_sq_mm, tn_sd, tn_rec, tn_mm, tn_out = (sem(n) for n in (
            "tn_sq", "tn_sq_mm", "tn_sd", "tn_rec", "tn_mm", "tn_out"))
        TNORMS = {}
        for name, tiles, blocks, scale in (("gdn_qk", range(GQ0, GQ0 + 8), 1, 1.0),
                                           ("even_out", [4, 5, 6, 7, 0, 1, 2, 3], 1, 1.0 / RDV),
                                           ("odd_qk", range(0, 10), 2, 1.0 / HD)):
            TNORMS[name] = (list(tiles), blocks, scale, sum(len(v[0]) for v in TNORMS.values()), len(TNORMS))

        def act_tnorm(act, name):
            tiles, blocks, scale, u, n = TNORMS[name]
            for j, t in enumerate(tiles):
                if u + j >= 2:
                    act.wait_ge(tn_sq_mm, u + j - 1)
                nc.scalar.activation(tmp_a[j % 2][:, :], proj[:, t, :], ACT.Square).then_inc(tn_sq, 1)
            act.wait_ge(tn_sq_mm, u + len(tiles))
            m = len(tiles) * TT * blocks
            nc.scalar.activation(stat_sd[:, 0:m], ps[:, 0, 0:m], ACT.Sqrt, bias=eps[:, :], scale=scale).then_inc(tn_sd, 1)

        def pe_tnorm_sums(pe, name):
            tiles, blocks, scale, u, n = TNORMS[name]
            for j in range(len(tiles)):
                pe.wait_ge(tn_sq, u + j + 1)
                for b in range(TT):
                    o = (j * TT + b) * blocks
                    mm = nc.tensor.matmul(ps[:, 0, o:o + blocks], tmp_a[j % 2][:, b * P:(b + 1) * P],
                                          ones[:, 0:1] if blocks == 1 else halves[:, :], start=True, stop=True)
                mm.then_inc(tn_sq_mm, 1)

        def tn_banks(j):
            o = (2 + 2 * (j % 3)) * 512
            return o

        def dve_tnorm_rec(dve, name):
            tiles, blocks, scale, u, n = TNORMS[name]
            m = len(tiles) * TT * blocks
            dve.wait_ge(tn_sd, n + 1)
            nc.vector.reciprocal(stat_r[:, 0:m], stat_sd[:, 0:m]).then_inc(tn_rec, 1)

        def pe_tnorm_spread(pe, name, rec_count):
            tiles, blocks, scale, u, n = TNORMS[name]
            pe.wait_ge(tn_rec, rec_count)
            for j in range(len(tiles)):
                if j >= 3:
                    pe.wait_ge(tn_out, u + j - 2)
                for b in range(TT):
                    c = (j * TT + b) * blocks
                    o = tn_banks(j) + b * P
                    m = P // blocks
                    for k in range(blocks):
                        mm = nc.tensor.matmul(psf[k * m:(k + 1) * m, o:o + P], stat_r[:, c + k:c + k + 1].to_broadcast([P, m]),
                                              ident[:, :], start=True, stop=True)
                mm.then_inc(tn_mm, 1)

        ab_raw = const("ab_raw", [P, KT, 16])
        ab_hi = const("ab_hi", [P, KT, 16], F32R)
        ab_lo = const("ab_lo", [P, KT, 16], F32R)
        heads_in = const("heads_in", [P, 3, 8])
        norm_cols = const("norm_cols", [P, 2])
        ab = const("ab", [P, TT, 16])
        spx = const("spx", [P, 48])
        spa = const("spa", [P, 48])
        exp_a = const("exp_a", [P, 8])
        beta = const("beta", [P, TT, 8])
        g_tok = const("g_tok", [P, TT, 8])
        lg = const("lg", [P, 8])
        lgp = const("lgp", [P, 2, 2])
        gcum = const("gcum", [P, 2, TT, GH])
        gsum = const("gsum", [P, 2, TT, GH])
        neg_e = const("neg_e", [P, 2, TT, GH])
        k_fac = const("k_fac", [P, 2, TT, GH])
        s_fac = const("s_fac", [P, 2, TT, GH])
        kr_fac = const("kr_fac", [P, 8])
        g_st = const("g_st", [P, 2, GH])

        def over_h(name, shape, offset, dt=F32):
            return at(name, shape, o_h + offset, dt)

        dist = over_h("dist", [P, 2, STRIP], 0)
        strip = [over_h(f"strip{s}", [P, STRIP], 7168 + s * 3584) for s in range(2)]
        pos = over_h("pos", [P, 2, NLAT], 14336)
        qd = over_h("qd", [P, 2, 2, NLAT], 18432)
        sc = [over_h(f"sc{s}", [P, NLAT], 26624 + s * 2048) for s in range(2)]
        s0r = over_h("s0r", [P, 2, 2, RDV], 30720)
        kdt = over_h("kdt", [P, 2, 256], 32768)
        sro = over_h("sro", [RDK, 8, RDV], 34816)

        names = ("kst", "e", "attn", "mt", "lm", "x_", "xt", "pm", "qdec")
        gb = [{n: over_h(f"gdn_{n}{d}", [P, GH, P], (9 * d + k) * 2048) for k, n in enumerate(names)} for d in range(2)]
        gs = [over_h(f"gdn_s{d}", [P, GH, P], (18 + d) * 2048) for d in range(2)]

        small_in, ab_in = sem("small_in"), sem("ab_in")
        ab_hi_ready, ab_lo_ready, ab_mm = sem("ab_hi_ready"), sem("ab_lo_ready"), sem("ab_mm")
        gate_dve, gate_act, cum_mm = sem("gate_dve"), sem("gate_act"), sem("cum_mm")
        conv_step, mix_silu = sem("conv_step"), sem("mix_silu")
        ret_in, gdn_in = sem("ret_in"), sem("gdn_in")
        k_scaled, vt_mm, vt_out, kc_mm, kdt_ready = (sem(n) for n in ("k_scaled", "vt_mm", "vt_out", "kc_mm", "kdt_ready"))
        krf_ready, qd_exp, qd_ready, strip_lin, strip_exp, strip_ready = (sem(n) for n in (
            "krf_ready", "qd_exp", "qd_ready", "strip_lin", "strip_exp", "strip_ready"))
        sc_mm, sc_ready, sc_used, o_out, sr_mm, sr_out = (sem(n) for n in (
            "sc_mm", "sc_ready", "sc_used", "o_out", "sr_mm", "sr_out"))
        mo_full, mo_gated, mo_hi, mo_lo = (sem(n) for n in ("mo_full", "mo_gated", "mo_hi", "mo_lo"))
        sr_stored = sem("sr_stored")
        SEGS = ((0, 2, "plain"), (4, 1, "silu"), (6, 3, "conv"), (12, 1, "silu"))

        def sp_even(sp):
            for r, v in enumerate((ins["ret_decay_logit"], ins["gdn_A_log"], ins["gdn_dt_bias"])):
                src = v.rearrange("e d h -> e (d h)").to_broadcast([P, 8])
                sp.dma_start(heads_in[:, r, :], src).then_inc(small_in, 16)
            for r, v in enumerate((ins["ret_norm_w"], ins["gdn_norm_w"])):
                sp.dma_start(norm_cols[:, r:r + 1], v.rearrange("e n -> n e")).then_inc(small_in, 16)
            w = ins["even_w_in"][0]
            sp.dma_start(ab_raw[:, :, :], w[:, 3584:3600].rearrange("(k p) n -> p k n", p=P)).then_inc(ab_in, 16)
            sp_linear(sp, "even_in", w[:, 0:3584], 14)
            sp_linear(sp, "even_out", ins["even_w_out"][0], 4)
            sp.wait_ge(ab_mm, 1)
            sp.dma_start(dist[:, :, :], ins["c_dist"]).then_inc(ret_in, 16)
            sp.dma_start(pos[:, :, :], ins["c_pos"]).then_inc(ret_in, 16)
            for half in range(2):
                for t in range(2):
                    sp.dma_start(s0r[half * RDK:(half + 1) * RDK, t, :, :],
                                 ins["state_ret"][0, 0, :, 2 * t + half].rearrange("d k v -> k d v")).then_inc(ret_in, 16)
            sp.wait_ge(sr_out, 2)
            sp.dma_start(outs["new_state_ret"][0, 0].rearrange("d h k v -> k (d h) v"), sro[:, :, :]).then_inc(out_done, 16)
            sp.wait_ge(out_done, 16)
            sp.sem_inc(sr_stored, 1)
            sp.wait_ge(o_out, RH)
            for d in range(2):
                sp.dma_start(gs[d][:, :, :], ins["state_gdn"][0, 0, d].rearrange("h k v -> k h v")).then_inc(gdn_in, 16)
            for d in range(2):
                gdn_wait(sp, "s_ready", d, 5)
                sp.dma_start(outs["new_state_gdn"][0, 0, d].rearrange("h k v -> k h v"), gs[d][:, :, :]).then_inc(out_done, 16)
            sp.wait_ge(out_done, 48)
            sp.sem_inc(gs_stored, 1)

        def dve_even_in(dve):
            g0 = GROUPS["even_in"]
            for first, bodies, kind in SEGS:
                def body(i):
                    for s in range(2):
                        r = first + 2 * i + s
                        g = g0 + r
                        if kind != "conv":
                            dve_take_group(dve, g, s, 2 * r)
                            dve_split(dve, g + 2, s)
                            continue
                        c0 = 10 * (r - 6)
                        dve.wait_ge(group_mm, g + 1)
                        if not isinstance(i, int) or 2 * i + s > 0:
                            dve.wait_ge(conv_step, c0)
                        for n in range(2):
                            cp = nc.vector.tensor_copy(tmp_b[n][:, :].rearrange("p (b n) -> p b n", b=2),
                                                       ps[:, 4 * s + 2 * n:4 * s + 2 * n + 2, 0:HALF])
                        cp.then_inc(group_out, 1)
                        dve_split(dve, g + 2, s)
                        dve.wait_ge(group_out, g + 1)
                        w0 = ROWS["conv"] + 2 * (r - 6)

                        def y(n, c0_, c1_):
                            return proj[:, ds(2 * r + n, 1), c0_:c1_]

                        def v(n, c0_, c1_):
                            return tmp_b[n][:, c0_:c1_].unsqueeze(1)

                        for n in range(2):
                            nc.vector.tensor_scalar(y(n, 0, T), v(n, 0, T), vecs[:, ds(w0 + 12 + n, 1)], None,
                                                    ALU.mult).then_inc(conv_step, 1)
                        for step, off, cols in ((0, 0, ((1, NCTX), (NCTX + 1, T))), (1, 24, ((0, NCTX - 1), (NCTX, T - 1)))):
                            for n in range(2):
                                dve.wait_ge(conv_step, c0 + (n + 1 if step == 0 else 4 + 2 * n))
                                for a_, b_ in cols:
                                    sh = -1 if step == 0 else 1
                                    nc.vector.scalar_tensor_tensor(y(n, a_, b_), v(n, a_ + sh, b_ + sh),
                                                                   vecs[:, ds(w0 + off + n, 1)], y(n, a_, b_),
                                                                   ALU.mult, ALU.add).then_inc(conv_step, 1)

                if kind == "conv":
                    body(0)
                    with dve.Fori(1, bodies) as i:
                        body(i)
                else:
                    body_loop(dve, g0 + first, bodies, body)

        def act_even_in(act):
            g0 = GROUPS["even_in"]
            for first, bodies, kind in SEGS:
                def body(i):
                    for s in range(2):
                        r = first + 2 * i + s
                        act_split(act, g0 + r + 2, s)
                        if kind == "plain":
                            continue
                        if kind == "silu":
                            act.wait_ge(group_out, g0 + r + 1)
                        else:
                            act.wait_ge(conv_step, 10 * (r - 6) + 10)
                        v = proj[:, ds(2 * r, 2), :]
                        nc.scalar.activation(v, v, ACT.Silu).then_inc(mix_silu, 1)

                body_loop(act, g0 + first, bodies, body)

        def pe_ab(pe):
            pe.wait_ge(ab_lo_ready, 1)
            pe.wait_ge(group_out, GROUPS["even_in"] + 14)
            for b in range(TT):
                for k in range(KT):
                    for v, w, first, last in ((h_hi, ab_hi, True, False), (h_lo, ab_hi, False, False), (h_hi, ab_lo, False, True)):
                        mm = nc.tensor.matmul(ps[:, 0, 16 * b:16 * b + 16], v[:, k, b * P:(b + 1) * P], w[:, k, :],
                                              start=(first and k == 0), stop=(last and k == KT - 1))
            mm.then_inc(ab_mm, 1)

        def dve_gates(dve):
            dve.wait_ge(ab_mm, 1)
            dve.wait_ge(small_in, 80)
            nc.vector.tensor_copy(ab[:, :, :], ps[:, 0, 0:16 * TT].rearrange("p (t c) -> p t c", t=TT)).then_inc(gate_dve, 1)
            nc.vector.tensor_scalar(spx[:, 40:48], heads_in[:, 0, :], -1.0, None, ALU.mult).then_inc(gate_dve, 1)
            dve.wait_ge(gate_dve, 2)
            nc.vector.tensor_tensor(spx[:, 0:40].rearrange("p (t c) -> p t c", t=TT), ab[:, :, 0:8],
                                    heads_in[:, 2:3, :].to_broadcast([P, TT, 8]), ALU.add).then_inc(gate_dve, 1)
            dve.wait_ge(gate_dve, 3)
            nc.vector.scalar_tensor_tensor(spa[:, :], spx[:, :], -1.0, spx[:, :], ALU.mult, ALU.max).then_inc(gate_dve, 1)
            dve.wait_ge(gate_act, 4)
            nc.vector.scalar_tensor_tensor(spx[:, :], spx[:, :], 0.0, spa[:, :], ALU.max, ALU.add).then_inc(gate_dve, 1)
            nc.vector.tensor_scalar(beta[:, :, :], beta[:, :, :], 1.0, None, ALU.add).then_inc(gate_dve, 1)
            dve.wait_ge(gate_dve, 6)
            nc.vector.reciprocal(beta[:, :, :], beta[:, :, :]).then_inc(gate_dve, 1)
            nc.vector.scalar_tensor_tensor(g_tok[:, :, :], spx[:, 0:40].rearrange("p (t c) -> p t c", t=TT), -1.0,
                                           exp_a[:, :].unsqueeze(1).to_broadcast([P, TT, 8]),
                                           ALU.mult, ALU.mult).then_inc(gate_dve, 1)
            nc.vector.tensor_scalar(lg[:, :], spx[:, 40:48], -1.0, None, ALU.mult).then_inc(gate_dve, 1)
            dve.wait_ge(gate_dve, 9)
            for half in range(2):
                q = slice(half * 64, half * 64 + 64)
                nc.vector.tensor_copy(lgp[q, :, :], lg[q, :].rearrange("p (d t h) -> p h t d", d=2, h=2)[:, half]).then_inc(gate_dve, 1)
            dve.wait_ge(cum_mm, 1)
            nc.vector.tensor_copy(gcum[:, :, :, :].rearrange("p d t h -> p (d t h)"), ps[:, 1, 0:40]).then_inc(gate_dve, 1)
            for d in range(2):
                nc.vector.tensor_copy(gsum[:, d, :, :], ps[:, 1, 64:104].rearrange("p (t d h) -> p d t h", t=TT, d=2)[:, d]).then_inc(gate_dve, 1)
            dve.wait_ge(gate_dve, 14)
            nc.vector.tensor_tensor(k_fac[:, :, :, :], gsum[:, :, :, :], gcum[:, :, :, :], ALU.subtract).then_inc(gate_dve, 1)
            dve.wait_ge(gate_act, 7)
            nc.vector.tensor_scalar(neg_e[:, :, :, :], neg_e[:, :, :, :], -1.0, None, ALU.mult).then_inc(gate_dve, 1)

        def act_gates(act):
            act.wait_ge(gate_dve, 4)
            nc.scalar.activation(spa[:, :], spa[:, :], ACT.Exp, scale=-1.0).then_inc(gate_act, 1)
            nc.scalar.activation(beta[:, :, :], ab[:, :, 8:16], ACT.Exp, scale=-1.0).then_inc(gate_act, 1)
            nc.scalar.activation(exp_a[:, :], heads_in[:, 1, :], ACT.Exp).then_inc(gate_act, 1)
            act.wait_ge(gate_act, 3)
            nc.scalar.activation(spa[:, :], spa[:, :], ACT.Ln, bias=1.0).then_inc(gate_act, 1)
            act.wait_ge(gate_dve, 15)
            nc.scalar.activation(neg_e[:, :, :, :], gcum[:, :, :, :], ACT.Exp).then_inc(gate_act, 1)
            nc.scalar.activation(k_fac[:, :, :, :], k_fac[:, :, :, :], ACT.Exp).then_inc(gate_act, 1)
            nc.scalar.activation(s_fac[:, :, :, :], gsum[:, :, :, :], ACT.Exp).then_inc(gate_act, 1)

        def pe_cum(pe):
            pe.wait_ge(gate_dve, 9)
            for d in range(2):
                nc.tensor.matmul(ps[:, 1, 20 * d:20 * d + 20], tri[:, d, :], g_tok[:, :, GH * d:GH * d + GH], start=True, stop=True)
            nc.tensor.matmul(ps[:, 1, 64:104], ones[:, :], g_tok[:, :, :], start=True, stop=True).then_inc(cum_mm, 1)

        def pe_values(pe):
            pe.wait_ge(mix_silu, 10)
            pe.wait_ge(k_scaled, 1)
            for u in range(2 * TT):
                tile, b = (RV0, u) if u < TT else (GV0, u - TT)
                if u >= 4:
                    pe.wait_ge(vt_out, u - 3)
                for h in range(4):
                    mm = nc.tensor.transpose(ps[:, 2 + u % 4, h * P:(h + 1) * P], proj[:, tile + h, b * P:(b + 1) * P], ident[:, :])
                mm.then_inc(vt_mm, 1)
            for t in range(2):
                mm = nc.tensor.transpose(ps[:, 6, t * P:(t + 1) * P], proj[:, RK0 + t, 0:P], ident[:, :])
            mm.then_inc(kc_mm, 1)

        def act_values(act):
            for u in range(2 * TT):
                tile, b = (RV0, u) if u < TT else (GV0, u - TT)
                act.wait_ge(vt_mm, u + 1)
                nc.scalar.copy(proj[:, tile:tile + 4, b * P:(b + 1) * P],
                               ps[:, 2 + u % 4, :].rearrange("p (h n) -> p h n", h=4)).then_inc(vt_out, 1)

        def act_ret(act):
            act.wait_ge(ret_in, 96)
            act.wait_ge(gate_dve, 11)
            for d in range(2):
                col = dist[:, 0, 511:512] if d == 0 else dist[:, 1, 384:385]
                nc.scalar.activation(kr_fac[:, 4 * d:4 * d + 4], lg[:, 4 * d:4 * d + 4], ACT.Exp, scale=col).then_inc(krf_ready, 1)
            for t in range(2):
                for d in range(2):
                    nc.scalar.activation(qd[:, t, d, :], pos[:, d, :], ACT.Exp, scale=lgp[:, t, d:d + 1]).then_inc(qd_exp, 1)
            for h in range(RH):
                act.wait_ge(strip_lin, 2 * h + 2)
                nc.scalar.activation(strip[h % 2][:, :], strip[h % 2][:, :], ACT.Exp).then_inc(strip_exp, 1)
            for k in range(2):
                act.wait_ge(sr_mm, 1)
                nc.scalar.copy(sro[:, 4 * k:4 * k + 4, :].rearrange("p h n -> p (h n)"), ps[0:RDK, 6 + k, :]).then_inc(sr_out, 1)

        def dve_ret(dve):
            dve.wait_ge(krf_ready, 2)
            dve.wait_ge(kc_mm, 1)
            for d in range(2):
                for h in range(RH):
                    kd = nc.vector.tensor_scalar(kdt[:, d, h * RDK:(h + 1) * RDK], ps[:, 6, h * RDK:(h + 1) * RDK],
                                                 kr_fac[:, 4 * d + h:4 * d + h + 1], None, ALU.mult)
            kd.then_inc(kdt_ready, 1)
            for t in range(2):
                for d in range(2):
                    dve.wait_ge(qd_exp, 2 * t + d + 1)
                    nc.vector.tensor_tensor(qd[:, t, d, :], qd[:, t, d, :], proj[:, RQ0 + t, NCTX:T], ALU.mult).then_inc(qd_ready, 1)
            for h in range(RH):
                if h >= 2:
                    dve.wait_ge(sc_ready, 5 * (h - 1))
                nc.vector.tensor_scalar(strip[h % 2][:, :], dist[:, 1, :], lg[:, 4 + h:5 + h], None, ALU.mult).then_inc(strip_lin, 1)
                dve.wait_ge(strip_lin, 2 * h + 1)
                nc.vector.scalar_tensor_tensor(strip[h % 2][:, :], dist[:, 0, :], lg[:, h:h + 1], strip[h % 2][:, :],
                                               ALU.mult, ALU.add).then_inc(strip_lin, 1)
                dve.wait_ge(strip_exp, h + 1)
                nc.vector.tensor_tensor(strip[h % 2][:, 384:512], strip[h % 2][:, 384:512], ident[:, :], ALU.add).then_inc(strip_ready, 1)
                dve.wait_ge(strip_ready, h + 1)
                for i in range(TT):
                    n = TT * h + i
                    dve.wait_ge(sc_mm, n + 1)
                    if n >= 2:
                        dve.wait_ge(sc_used, n - 1)
                    w = P if i == 0 else NLAT
                    o = 384 if i == 0 else 384 - P * (i - 1)
                    nc.vector.tensor_tensor(sc[n % 2][:, 0:w], ps[:, 1 + n % 2, 0:w], strip[h % 2][:, o:o + w],
                                            ALU.mult).then_inc(sc_ready, 1)
                dve.wait_ge(sc_used, TT * (h + 1))
                nc.vector.tensor_copy(proj[:, RV0 + h, 0:NCTX], ps[:, 3, 0:NCTX])
                nc.vector.tensor_copy(proj[:, RV0 + h, NCTX:T], ps[:, 4, :]).then_inc(o_out, 1)

        def pe_ret(pe):
            pe.wait_ge(kdt_ready, 1)
            pe.wait_ge(vt_out, 2 * TT)
            for d in range(2):
                for h in range(RH):
                    mm = nc.tensor.matmul(ps[0:RDK, 6 + d, h * RDV:(h + 1) * RDV], kdt[:, d, h * RDK:(h + 1) * RDK],
                                          proj[:, RV0 + h, 0:P], start=True, stop=True)
            mm.then_inc(sr_mm, 1)
            pe.wait_ge(k_scaled, 1)
            pe.wait_ge(qd_ready, 4)

            def scores(n):
                h, i = n // TT, n % TT
                q = slice(64 * (h % 2), 64 * (h % 2) + 64)
                if n >= 2:
                    pe.wait_ge(sc_ready, n - 1)
                c0, c1 = (0, NCTX) if i == 0 else (NCTX, T)
                nc.tensor.matmul(ps[:, 1 + n % 2, 0:c1 - c0], proj[q, RK0 + h // 2, i * P:(i + 1) * P],
                                 proj[q, RQ0 + h // 2, c0:c1], start=True, stop=True).then_inc(sc_mm, 1)

            scores(0)
            for n in range(TT * RH):
                h, i = n // TT, n % TT
                if n + 1 < TT * RH:
                    scores(n + 1)
                if i == 0:
                    if h:
                        pe.wait_ge(o_out, h)
                    q = slice(64 * (h % 2), 64 * (h % 2) + 64)
                    for d in range(2):
                        nc.tensor.matmul(ps[:, 4, :], s0r[q, h // 2, d, :], qd[q, h // 2, d, :], start=(d == 0), stop=False)
                pe.wait_ge(sc_ready, n + 1)
                out = ps[:, 3, 0:NCTX] if i == 0 else ps[:, 4, :]
                mm = nc.tensor.matmul(out, proj[:, RV0 + h, i * P:(i + 1) * P], sc[n % 2][:, 0:(P if i == 0 else NLAT)],
                                      start=(i == 0), stop=(i in (0, TT - 1)))
                mm.then_inc(sc_used, 1)

        STEPS = {"prep_mm": ("rows_mm", "kk_mm", "kq_mm", "kt_mm"),
                 "prep_ready": ("diff_ready", "mt_ready", "attn_raw", "kd_ready"),
                 "exp_ready": ("e_ready", "row_exp"),
                 "mask_ready": ("attn_ready", "qdec_ready"),
                 "scan_mm": ("ks_mm", "y_mm2", "su_mm", "oo_mm"),
                 "scan_ready": ("r_ready2", "y_ready", "s_ready", "o_added")}
        gnames = ("g_staged", "k_staged", "lm_ready", "p_mm", "p_ready", "xx_mm", "x_ready", "xt_ready") + tuple(STEPS)
        ev = {n: [sem(f"gdn_{n}{d}") for d in range(2)] for n in gnames}
        PLACE = {e: (name, len(events), k + 1) for name, events in STEPS.items() for k, e in enumerate(events)}

        def gdn_sem(event, d):
            return ev[PLACE[event][0]][d]

        def gdn_wait(eng, event, d, count):
            name, per, k = PLACE[event]
            eng.wait_ge(ev[name][d], per * count + (k - per))

        gs_stored, o_zero, s_zero = sem("gs_stored"), sem("o_zero"), sem("s_zero")
        NL = len(LEVELS)

        def gdn_loop(eng, body):
            body(0, (1, 4))
            with eng.Fori(1, 4) as n:
                body(n, (n + 1, n * -1 + 4))
            body(4, (0, 0))

        def head(v, h):
            return v[:, h, :]

        def act_gdn(act):
            def body(n, tiles):
                for d in range(2):
                    if isinstance(n, int) and n == 0 and d == 0:
                        act.wait_ge(sc_used, TT * RH)
                        act.wait_ge(sr_stored, 1)
                        act.wait_ge(tn_out, 8)
                    if not isinstance(n, int) or n > 0:
                        gdn_wait(act, "su_mm", d, n)
                        gdn_wait(act, "oo_mm", d, n)
                    nc.scalar.copy(gb[d]["kst"][:, :, :], proj[:, GK0:GK0 + GH, ds(tiles[d] * P, P)]).then_inc(ev["k_staged"][d], 1)
                for d in range(2):
                    gdn_wait(act, "diff_ready", d, n + 1)
                    nc.scalar.activation(gb[d]["e"][:, :, :], gb[d]["e"][:, :, :], ACT.Exp).then_inc(gdn_sem("e_ready", d), 1)
                    nc.scalar.activation(gb[d]["qdec"][:, :, :], ps[:, 4 * d, :].rearrange("p (h n) -> p h n", h=GH),
                                         ACT.Exp).then_inc(gdn_sem("row_exp", d), 1)
                for l in range(1, NL):
                    for d in range(2):
                        act.wait_ge(ev["p_mm"][d], NL * n + l + 1)
                        nc.scalar.copy(gb[d]["pm"][:, :, :], ps[:, 4 * d + 1, :].rearrange("p (h n) -> p h n", h=GH))\
                            .then_inc(ev["p_ready"][d], 1)

            gdn_loop(act, body)

        def pool_gdn(pool):
            def body(n, tiles):
                for l in range(NL):
                    for d in range(2):
                        b = gb[d]
                        if l == 0:
                            gdn_wait(pool, "mt_ready", d, n + 1)
                            if not isinstance(n, int) or n > 0:
                                gdn_wait(pool, "y_mm2", d, n)
                        else:
                            pool.wait_ge(ev["p_mm"][d], NL * n + l)
                        if l == 1:
                            pool.wait_ge(ev["xt_ready"][d], NL * n + 1)
                        nc.gpsimd.tensor_tensor(b["lm"][:, :, :], b["mt"][:, :, :],
                                                lvl[:, d, l:l + 1, :].to_broadcast([P, GH, P]), ALU.mult).then_inc(ev["lm_ready"][d], 1)
                        if l == 1:
                            gdn_wait(pool, "attn_raw", d, n + 1)
                            nc.gpsimd.tensor_tensor(b["attn"][:, :, :], b["attn"][:, :, :],
                                                    tri[:, d:d + 1, :].to_broadcast([P, GH, P]), ALU.mult).then_inc(gdn_sem("attn_ready", d), 1)
                        if l == 2:
                            gdn_wait(pool, "row_exp", d, n + 1)
                            nc.gpsimd.tensor_tensor(b["qdec"][:, :, :], b["qdec"][:, :, :],
                                                    proj[:, GQ0:GQ0 + GH, ds(tiles[d] * P, P)], ALU.mult).then_inc(gdn_sem("qdec_ready", d), 1)

            gdn_loop(pool, body)

        def dve_gdn(dve):
            def body(n, tiles):
                for d in range(2):
                    if not isinstance(n, int) or n > 0:
                        gdn_wait(dve, "rows_mm", d, n)
                    nc.vector.tensor_copy(g_st[:, d:d + 1, :], g_tok[:, ds(tiles[d], 1), GH * d:GH * d + GH]).then_inc(ev["g_staged"][d], 1)
                for d in range(2):
                    b = gb[d]
                    gdn_wait(dve, "rows_mm", d, n + 1)
                    for h in range(GH):
                        v = nc.vector.tensor_scalar(head(b["e"], h), ps[:, 4 * d, h * P:(h + 1) * P],
                                                    gcum[:, d, ds(tiles[d], 1), h:h + 1], 0.0, ALU.subtract, ALU.min)
                    v.then_inc(gdn_sem("diff_ready", d), 1)
                for d in range(2):
                    b = gb[d]
                    gdn_wait(dve, "e_ready", d, n + 1)
                    gdn_wait(dve, "kk_mm", d, n + 1)
                    for h in range(GH):
                        v = nc.vector.scalar_tensor_tensor(head(b["mt"], h), head(b["e"], h), beta[:, ds(tiles[d], 1), GH * d + h:GH * d + h + 1],
                                                           ps[:, 4 * d + 1, h * P:(h + 1) * P], ALU.mult, ALU.mult)
                    v.then_inc(gdn_sem("mt_ready", d), 1)
                    gdn_wait(dve, "kq_mm", d, n + 1)
                    nc.vector.tensor_tensor(b["attn"][:, :, :], b["e"][:, :, :],
                                            ps[:, 4 * d + 2, :].rearrange("p (h n) -> p h n", h=GH), ALU.mult).then_inc(gdn_sem("attn_raw", d), 1)
                    gdn_wait(dve, "kt_mm", d, n + 1)
                    gdn_wait(dve, "attn_raw", d, n + 1)
                    for h in range(GH):
                        v = nc.vector.tensor_scalar(head(b["e"], h), ps[:, 4 * d + 3, h * P:(h + 1) * P],
                                                    k_fac[:, d, ds(tiles[d], 1), h:h + 1], None, ALU.mult)
                    v.then_inc(gdn_sem("kd_ready", d), 1)
                eye = ident[:, :].unsqueeze(1).to_broadcast([P, GH, P])
                for l in range(NL):
                    for d in range(2):
                        b = gb[d]

                        def bank(k):
                            return ps[:, 4 * d + k, :].rearrange("p (h n) -> p h n", h=GH)

                        if l == 0:
                            dve.wait_ge(ev["lm_ready"][d], NL * n + 1)
                            nc.vector.tensor_tensor(b["xt"][:, :, :], eye, b["lm"][:, :, :], ALU.subtract).then_inc(ev["xt_ready"][d], 1)
                            dve.wait_ge(ev["p_mm"][d], NL * n + 1)
                            nc.vector.tensor_tensor(b["x_"][:, :, :], eye, bank(1), ALU.subtract).then_inc(ev["x_ready"][d], 1)
                            continue
                        dve.wait_ge(ev["xx_mm"][d], (NL - 1) * n + l)
                        if l < NL - 1:
                            dve.wait_ge(ev["x_ready"][d], (NL - 1) * n + l)
                            nc.vector.tensor_tensor(b["x_"][:, :, :], b["x_"][:, :, :], bank(2), ALU.subtract).then_inc(ev["x_ready"][d], 1)
                        dve.wait_ge(ev["xt_ready"][d], NL * n + l)
                        nc.vector.tensor_tensor(b["xt"][:, :, :], b["xt"][:, :, :], bank(3), ALU.subtract).then_inc(ev["xt_ready"][d], 1)
                for d in range(2):
                    b = gb[d]
                    gdn_wait(dve, "ks_mm", d, n + 1)
                    for h in range(GH):
                        v = nc.vector.scalar_tensor_tensor(head(b["lm"], h), ps[:, 4 * d, h * P:(h + 1) * P],
                                                           neg_e[:, d, ds(tiles[d], 1), h:h + 1],
                                                           proj[:, GV0 + h, ds(tiles[d] * P, P)], ALU.mult, ALU.add)
                    v.then_inc(gdn_sem("r_ready2", d), 1)
                for d in range(2):
                    b = gb[d]
                    gdn_wait(dve, "y_mm2", d, n + 1)
                    for h in range(GH):
                        v = nc.vector.tensor_scalar(head(b["pm"], h), ps[:, 4 * d + 1, h * P:(h + 1) * P],
                                                    beta[:, ds(tiles[d], 1), GH * d + h:GH * d + h + 1], None, ALU.mult)
                    v.then_inc(gdn_sem("y_ready", d), 1)
                for d in range(2):
                    b = gb[d]
                    if isinstance(n, int) and n == 0:
                        dve.wait_ge(gdn_in, 32)
                        if d == 0:
                            dve.wait_ge(sc_used, TT * RH)
                            nc.vector.memset(proj[:, 0:GH, :], 0.0).then_inc(o_zero, 1)
                            dve.wait_ge(o_zero, 1)
                    gdn_wait(dve, "su_mm", d, n + 1)
                    for h in range(GH):
                        v = nc.vector.scalar_tensor_tensor(head(gs[d], h), head(gs[d], h), s_fac[:, d, ds(tiles[d], 1), h:h + 1],
                                                           ps[:, 4 * d + 3, h * P:(h + 1) * P], ALU.mult, ALU.add)
                    v.then_inc(gdn_sem("s_ready", d), 1)
                    gdn_wait(dve, "oo_mm", d, n + 1)
                    if d == 1:
                        gdn_wait(dve, "o_added", 0, n + 1)
                    if not isinstance(n, int) or n > 0:
                        gdn_wait(dve, "o_added", 1, n)
                    o = proj[:, 0:GH, ds(tiles[d] * P, P)]
                    nc.vector.tensor_tensor(o, o, ps[:, 4 * d + 2, :].rearrange("p (h n) -> p h n", h=GH), ALU.add).then_inc(gdn_sem("o_added", d), 1)

            body(0, (1, 4))
            with dve.Fori(1, 4) as n:
                body(n, (n + 1, n * -1 + 4))
            for d in range(2):
                gdn_wait(dve, "s_ready", d, 4)
                nc.vector.memset(gs[d][:, :, :], 0.0).then_inc(s_zero, 1)
            body(4, (0, 0))

        def pe_gdn(pe):
            def body(n, tiles):
                for d in range(2):
                    b = gb[d]
                    pe.wait_ge(ev["g_staged"][d], n + 1)
                    pe.wait_ge(ev["k_staged"][d], n + 1)
                    if isinstance(n, int) and n == 0:
                        pe.wait_ge(sr_out, 2)
                        pe.wait_ge(o_out, RH)
                        pe.wait_ge(sc_ready, TT * RH)
                    else:
                        gdn_wait(pe, "o_added", d, n)
                        gdn_wait(pe, "s_ready", d, n)
                    for h in range(GH):
                        mm = nc.tensor.matmul(ps[:, 4 * d, h * P:(h + 1) * P], g_st[:, d, h:h + 1].to_broadcast([P, P]),
                                              tri[:, d, :], start=True, stop=True)
                    mm.then_inc(gdn_sem("rows_mm", d), 1)
                    for h in range(GH):
                        k = head(b["kst"], h)
                        mm = nc.tensor.matmul(ps[:, 4 * d + 1, h * P:(h + 1) * P], k, k, start=True, stop=True)
                    mm.then_inc(gdn_sem("kk_mm", d), 1)
                    for h in range(GH):
                        mm = nc.tensor.matmul(ps[:, 4 * d + 2, h * P:(h + 1) * P], head(b["kst"], h),
                                              proj[:, GQ0 + h, ds(tiles[d] * P, P)], start=True, stop=True)
                    mm.then_inc(gdn_sem("kq_mm", d), 1)
                    for h in range(GH):
                        mm = nc.tensor.transpose(ps[:, 4 * d + 3, h * P:(h + 1) * P], head(b["kst"], h), ident[:, :])
                    mm.then_inc(gdn_sem("kt_mm", d), 1)
                for l in range(NL):
                    for d in range(2):
                        b = gb[d]
                        pe.wait_ge(ev["lm_ready"][d], NL * n + l + 1)
                        if l >= 1:
                            pe.wait_ge(ev["x_ready"][d], (NL - 1) * n + l)
                        for h in range(GH):
                            mm = nc.tensor.matmul(ps[:, 4 * d + 1, h * P:(h + 1) * P], head(b["lm"], h),
                                                  ident[:, :] if l == 0 else head(b["x_"], h), start=True, stop=True)
                        mm.then_inc(ev["p_mm"][d], 1)
                    for d in range(2 if l else 0):
                        b = gb[d]
                        pe.wait_ge(ev["p_ready"][d], (NL - 1) * n + l)
                        pe.wait_ge(ev["xt_ready"][d], NL * n + l)
                        if l == 1:
                            gdn_wait(pe, "kd_ready", d, n + 1)
                        for h in range(GH if l < NL - 1 else 0):
                            nc.tensor.matmul(ps[:, 4 * d + 2, h * P:(h + 1) * P], head(b["xt"], h), head(b["pm"], h), start=True, stop=True)
                        for h in range(GH):
                            mm = nc.tensor.matmul(ps[:, 4 * d + 3, h * P:(h + 1) * P], head(b["pm"], h), head(b["xt"], h), start=True, stop=True)
                        mm.then_inc(ev["xx_mm"][d], 1)
                for d in range(2):
                    b = gb[d]
                    if isinstance(n, int) and n == 0:
                        pe.wait_ge(gdn_in, 32)
                    else:
                        gdn_wait(pe, "s_ready", d, n)
                    if isinstance(n, int) and n == 4:
                        pe.wait_ge(s_zero, 2)
                    gdn_wait(pe, "row_exp", d, n + 1)
                    for h in range(GH):
                        mm = nc.tensor.matmul(ps[:, 4 * d, h * P:(h + 1) * P], head(b["kst"], h), head(gs[d], h), start=True, stop=True)
                    mm.then_inc(gdn_sem("ks_mm", d), 1)
                    gdn_wait(pe, "qdec_ready", d, n + 1)
                    for h in range(GH):
                        nc.tensor.matmul(ps[:, 4 * d + 2, h * P:(h + 1) * P], head(gs[d], h), head(b["qdec"], h),
                                         start=(h == 0), stop=False, skip_group_check=True)
                for d in range(2):
                    b = gb[d]
                    gdn_wait(pe, "r_ready2", d, n + 1)
                    pe.wait_ge(ev["xt_ready"][d], NL * n + NL)
                    for h in range(GH):
                        mm = nc.tensor.matmul(ps[:, 4 * d + 1, h * P:(h + 1) * P], head(b["xt"], h), head(b["lm"], h), start=True, stop=True)
                    mm.then_inc(gdn_sem("y_mm2", d), 1)
                for d in range(2):
                    b = gb[d]
                    gdn_wait(pe, "y_ready", d, n + 1)
                    for h in range(GH):
                        mm = nc.tensor.matmul(ps[:, 4 * d + 3, h * P:(h + 1) * P], head(b["e"], h), head(b["pm"], h), start=True, stop=True)
                    mm.then_inc(gdn_sem("su_mm", d), 1)
                    gdn_wait(pe, "attn_ready", d, n + 1)
                    for h in range(GH):
                        mm = nc.tensor.matmul(ps[:, 4 * d + 2, h * P:(h + 1) * P], head(b["pm"], h), head(b["attn"], h),
                                              start=False, stop=(h == GH - 1), skip_group_check=True)
                    mm.then_inc(gdn_sem("oo_mm", d), 1)

            gdn_loop(pe, body)

        def act_even(act):
            act.wait_ge(ab_in, 16)
            nc.scalar.copy(ab_hi[:, :, :], ab_raw[:, :, :]).then_inc(ab_hi_ready, 1)
            act_even_in(act)
            act.wait_ge(group_out, GROUPS["even_in"] + 2)
            nc.scalar.mul(proj[:, RK0:RK0 + 2, :], proj[:, RK0:RK0 + 2, :], RDK ** -0.5).then_inc(k_scaled, 1)
            act_gates(act)
            act_tnorm(act, "gdn_qk")
            act_values(act)
            act_ret(act)
            act_gdn(act)
            act_tnorm(act, "even_out")
            for j in range(8):
                act.wait_ge(mo_gated, j + 1)
                if j == 0:
                    act.wait_ge(gs_stored, 1)
                nc.scalar.copy(h_hi[:, j, :], tmp_b[j % 2][:, :]).then_inc(mo_hi, 1)
            act_linear(act, "even_out", 4)

        def dve_even(dve):
            dve.wait_ge(ab_hi_ready, 1)
            nc.vector.tensor_tensor(ab_lo[:, :, :], ab_raw[:, :, :], ab_hi[:, :, :].bitcast(F32), ALU.subtract).then_inc(ab_lo_ready, 1)
            dve_even_in(dve)
            dve_gates(dve)
            dve_tnorm_rec(dve, "gdn_qk")
            dve.wait_ge(tn_rec, 1)
            nc.vector.tensor_scalar(stat_r[:, 0:4 * TT], stat_r[:, 0:4 * TT], GDK ** -0.5, None, ALU.mult).then_inc(tn_rec, 1)
            for j in range(8):
                dve.wait_ge(tn_mm, j + 1)
                nc.vector.tensor_tensor(proj[:, GQ0 + j, :], proj[:, GQ0 + j, :], psf[:, tn_banks(j):tn_banks(j) + T],
                                        ALU.mult).then_inc(tn_out, 1)
            dve_ret(dve)
            dve_gdn(dve)
            dve_tnorm_rec(dve, "even_out")
            dve_gate(dve, 1, 0, 1, 1.0, 12)
            for j, t in enumerate(TNORMS["even_out"][0]):
                dve.wait_ge(tn_mm, 8 + j + 1)
                if j >= 2:
                    dve.wait_ge(mo_lo, j - 1)
                nc.vector.scalar_tensor_tensor(tmp_b[j % 2][:, :], psf[:, tn_banks(j):tn_banks(j) + T],
                                               norm_cols[:, (0 if j < 4 else 1):(1 if j < 4 else 2)], proj[:, t, :],
                                               ALU.mult, ALU.mult).then_inc(tn_out, 1)
                dve.wait_ge(tn_out, 8 + j + 1)
                nc.vector.tensor_tensor(tmp_b[j % 2][:, :], tmp_b[j % 2][:, :], proj[:, (RG0 + j if j < 4 else GG0 + j - 4), :],
                                        ALU.mult).then_inc(mo_gated, 1)
                dve.wait_ge(mo_hi, j + 1)
                nc.vector.tensor_tensor(h_lo[:, j, :], tmp_b[j % 2][:, :], h_hi[:, j, :].bitcast(F32), ALU.subtract).then_inc(mo_lo, 1)
            dve_add_groups(dve, "even_out", 4, 1)

        def pool_even(pool):
            pool_gdn(pool)

        def pe_even(pe):
            pe_linear(pe, "even_in", 14, (hlo_ready, DT))
            pe_ab(pe)
            pe_cum(pe)
            pe_tnorm_sums(pe, "gdn_qk")
            pe_tnorm_spread(pe, "gdn_qk", 2)
            pe.wait_ge(tn_out, 8)
            pe_values(pe)
            pe_ret(pe)
            pe_gdn(pe)
            for d in range(2):
                gdn_wait(pe, "o_added", d, 5)
            pe_tnorm_sums(pe, "even_out")
            pe_tnorm_spread(pe, "even_out", 3)
            pe.wait_ge(tn_out, 16)
            pe_linear(pe, "even_out", 4, (mo_lo, 0))

        def over_u(name, shape, offset, dt=F32):
            return at(name, shape, o_u + 12 * TILE + offset, dt)

        KEYS = 2 * P + NLAT
        keys = over_u("keys", [P, KVH, KEYS], 0)
        vals = over_u("vals", [P, 6, KVH * HD], 12288)
        q_st = over_u("q_st", [P, DT, P], 18432)
        pt = [over_u(f"pt{s}", [P, 5 * P], 22528 + 2560 * s) for s in range(2)]
        pr = [over_u(f"pr{s}", [P, 5 * P], 27648 + 2560 * s) for s in range(2)]
        oq = over_u("oq", [P, D], 32768)
        k_out = over_u("k_out", [P, KVH * HD], 36864)
        a_max = over_u("a_max", [P, AH], 37888)
        a_neg = over_u("a_neg", [P, AH], 37952)
        a_den = over_u("a_den", [P, AH], 38016)
        a_rec = over_u("a_rec", [P, AH], 38080)
        rope = over_h("rope", [P, 2, NLAT], 0)
        swap = over_h("swap", [P, P], 4096)
        sel = over_h("sel", [P, 4, P], 4608)
        ck = over_h("ck", [P, KVH, HD], 6656)
        ckd = over_h("ckd", [P, KVH, 2, HD], 7680)
        rt = [over_h(f"rt{s}", [P, NLAT], 9728 + 2048 * s) for s in range(2)]
        halves = const("halves", [P, 2])
        qk_w = const("qk_w", [P, 2])

        oc_in, od_in, ckd_ready, ck_mm, ck_out = (sem(n) for n in ("oc_in", "od_in", "ckd_ready", "ck_mm", "ck_out"))
        kr_mm, kr_step, vo_mm, vo_out, ko_mm, ko_out = (sem(n) for n in ("kr_mm", "kr_step", "vo_mm", "vo_out", "ko_mm", "ko_out"))
        qr_mm, qr_step, kv_stored, q_staged = (sem(n) for n in ("qr_mm", "qr_step", "kv_stored", "q_staged"))
        at_s, at_max, at_neg, at_p, at_t, at_ta, at_td, at_o, at_rec, at_oq, at_ot, at_hi, at_lo = (sem("at_" + n) for n in (
            "s", "max", "neg", "p", "t", "ta", "td", "o", "rec", "oq", "ot", "hi", "lo"))
        K0, V0 = 8, 10
        ASCALE = HD ** -0.5

        def sp_odd(sp):
            sp.dma_start(halves[:, :], ins["c_half"]).then_inc(oc_in, 16)
            for r, v in enumerate((ins["q_norm_w"], ins["k_norm_w"])):
                for half in range(2):
                    sp.dma_start(qk_w[half * HD:(half + 1) * HD, r:r + 1], v.rearrange("e n -> n e")).then_inc(oc_in, 16)
            sp_linear(sp, "odd_in", ins["odd_w_in"][0], 6)
            sp_linear(sp, "odd_out", ins["odd_w_out"][0], 4)
            sp.wait_ge(group_mm, GROUPS["odd_in"] + 6)
            for dst, src in ((rope[:, :, :], ins["c_rope"]), (swap[:, :], ins["c_swap"]), (sel[:, :, :], ins["c_sel"]),
                             (ck[:, :, :], ins["cache_k"][0, 0]),
                             (vals[:, 1, :].rearrange("p (h d) -> p h d", h=KVH), ins["cache_v"][0, 0])):
                sp.dma_start(dst, src).then_inc(od_in, 16)
            sp.wait_ge(ko_out, 1)
            sp.dma_start(outs["new_cache_k"][0, 0], k_out[:, :].rearrange("p (h d) -> p h d", h=KVH)).then_inc(out_done, 16)
            sp.wait_ge(vo_out, 1)
            sp.dma_start(outs["new_cache_v"][0, 0], vals[:, 0, :].rearrange("p (h d) -> p h d", h=KVH)).then_inc(out_done, 16)
            sp.wait_ge(out_done, 80)
            sp.sem_inc(kv_stored, 1)

        def pe_odd_prep(pe):
            pe_tnorm_sums(pe, "odd_qk")
            pe_tnorm_spread(pe, "odd_qk", 4)
            pe.wait_ge(tn_out, 26)
            pe.wait_ge(od_in, 80)
            for b in range(TT):
                for t in range(2):
                    mm = nc.tensor.transpose(ps[:, b, t * P:(t + 1) * P], proj[:, V0 + t, b * P:(b + 1) * P], ident[:, :])
                mm.then_inc(vo_mm, 1)
            for t in range(2):
                mm = nc.tensor.transpose(ps[:, 5, t * P:(t + 1) * P], proj[:, K0 + t, 0:P], ident[:, :])
            mm.then_inc(ko_mm, 1)
            pe.wait_ge(ckd_ready, 1)
            for h in range(KVH):
                mm = nc.tensor.transpose(ps[:, 6, h * P:(h + 1) * P], ckd[:, h, :, :].rearrange("p a d -> p (a d)"), ident[:, :])
            mm.then_inc(ck_mm, 1)
            for h in range(KVH):
                pe.wait_ge(vo_out, TT)
                pe.wait_ge(ko_out, 1)
                if h >= 2:
                    pe.wait_ge(kr_step, 4 * (h - 1))
                o = (h % 2) * 3 * 512
                k = proj[:, K0 + h // 2, :]
                nc.tensor.matmul(psf[:, o:o + 512], sel[:, h % 2, :], k[:, 0:512], start=True, stop=True)
                nc.tensor.matmul(psf[:, o + 512:o + T], sel[:, h % 2, :], k[:, 512:T], start=True, stop=True)
                nc.tensor.matmul(psf[:, o + 1024:o + 1536], sel[:, 2 + h % 2, :], k[:, NCTX:T], start=True, stop=True).then_inc(kr_mm, 1)
            for j in range(DT):
                if j == 0:
                    pe.wait_ge(ck_out, 1)
                if j >= 2:
                    pe.wait_ge(qr_step, 3 * (j - 1))
                nc.tensor.matmul(ps[:, 6 + j % 2, :], swap[:, :], proj[:, j, NCTX:T], start=True, stop=True).then_inc(qr_mm, 1)

        def act_odd_prep(act):
            act.wait_ge(group_out, GROUPS["odd_in"] + 6)
            act_tnorm(act, "odd_qk")
            for b in range(TT):
                act.wait_ge(vo_mm, b + 1)
                nc.scalar.copy(vals[:, (b + 1 if b else 0), :], ps[:, b, 0:KVH * HD]).then_inc(vo_out, 1)
            act.wait_ge(ko_mm, 1)
            nc.scalar.copy(k_out[:, :], ps[:, 5, 0:KVH * HD]).then_inc(ko_out, 1)
            act.wait_ge(ck_mm, 1)
            nc.scalar.copy(keys[:, :, P:2 * P], ps[:, 6, :].rearrange("p (h n) -> p h n", h=KVH)).then_inc(ck_out, 1)

        def dve_odd_prep(dve):
            def take(i):
                for s in range(2):
                    g = GROUPS["odd_in"] + 2 * i + s
                    dve_take_group(dve, g, s, 4 * i + 2 * s)
                    dve_split(dve, g + 2, s)

            body_loop(dve, GROUPS["odd_in"], 3, take)
            dve.wait_ge(oc_in, 80)
            dve_tnorm_rec(dve, "odd_qk")
            for j in range(10):
                dve.wait_ge(tn_mm, 16 + j + 1)
                w = qk_w[:, 0:1] if j < K0 else qk_w[:, 1:2]
                nc.vector.scalar_tensor_tensor(proj[:, j, :], psf[:, tn_banks(j):tn_banks(j) + T], w, proj[:, j, :],
                                               ALU.mult, ALU.mult).then_inc(tn_out, 1)
            dve.wait_ge(od_in, 80)
            for a in range(2):
                cp = nc.vector.tensor_copy(ckd[:, :, a, :], ck[:, :, :])
            cp.then_inc(ckd_ready, 1)
            for h in range(KVH):
                o = (h % 2) * 3 * 512
                dve.wait_ge(kr_mm, h + 1)
                if h >= 2:
                    dve.wait_ge(kr_step, 4 * (h - 1))
                nc.vector.tensor_tensor(rt[h % 2][:, :], psf[:, o + 1024:o + 1536], rope[:, 1, :], ALU.mult).then_inc(kr_step, 1)
                nc.vector.tensor_copy(keys[:, h, 0:P], psf[:, o:o + P]).then_inc(kr_step, 1)
                nc.vector.tensor_tensor(keys[:, h, 2 * P:KEYS], psf[:, o + NCTX:o + T], rope[:, 0, :], ALU.mult).then_inc(kr_step, 1)
                dve.wait_ge(kr_step, 4 * h + 3)
                nc.vector.tensor_tensor(keys[:, h, 2 * P:KEYS], keys[:, h, 2 * P:KEYS], rt[h % 2][:, :], ALU.add).then_inc(kr_step, 1)
            for j in range(DT):
                q = proj[:, j, NCTX:T]
                dve.wait_ge(qr_mm, j + 1)
                if j < 2:
                    dve.wait_ge(kr_step, 16)
                else:
                    dve.wait_ge(qr_step, 3 * (j - 1))
                nc.vector.tensor_tensor(rt[j % 2][:, :], ps[:, 6 + j % 2, :], rope[:, 1, :], ALU.mult).then_inc(qr_step, 1)
                nc.vector.tensor_tensor(q, q, rope[:, 0, :], ALU.mult).then_inc(qr_step, 1)
                dve.wait_ge(qr_step, 3 * j + 2)
                nc.vector.tensor_tensor(q, q, rt[j % 2][:, :], ALU.add).then_inc(qr_step, 1)

        def blocks(eng, body):
            body(0, 1)
            with eng.Fori(1, TT) as n:
                body(n, 5)

        def after(eng, s, v):
            if not isinstance(v, int) or v > 0:
                eng.wait_ge(s, v)

        def pe_attention(pe):
            def body(n, kt):
                k0 = 0 if kt == 1 else P

                def scores(h):
                    u = AH * n + h
                    after(pe, at_p, u - 1)
                    q = slice(64 * (h % 2), 64 * (h % 2) + 64)
                    o = 2 * (h % 2) * 512
                    w = kt * P
                    for c in range(0, w, 512):
                        e = min(c + 512, w)
                        mm = nc.tensor.matmul(psf[:, o + c:o + e], q_st[q, h // 2, :], keys[q, h // 4, k0 + c:k0 + e],
                                              start=True, stop=True)
                    mm.then_inc(at_s, 1)

                def turn(h):
                    u = AH * n + h
                    pe.wait_ge(at_p, u + 1)
                    after(pe, at_ta, u)
                    after(pe, at_td, u)
                    for i in range(kt):
                        o = 4 * 512 + i * P
                        mm = nc.tensor.transpose(psf[:, o:o + P], pr[h % 2][:, i * P:(i + 1) * P], ident[:, :])
                    mm.then_inc(at_t, 1)

                def values(h):
                    u = AH * n + h
                    pe.wait_ge(at_ta, u + 1)
                    pe.wait_ge(at_td, u + 1)
                    after(pe, at_oq, u - 1)
                    for i in range(kt):
                        mm = nc.tensor.matmul(ps[:, 6 + h % 2, 0:HD], pt[h % 2][:, i * P:(i + 1) * P],
                                              vals[:, (0 if kt == 1 else 1 + i), (h // 4) * HD:(h // 4 + 1) * HD],
                                              start=(i == 0), stop=(i == kt - 1))
                    mm.then_inc(at_o, 1)

                pe.wait_ge(q_staged, n + 1)
                after(pe, at_lo, n)
                scores(0)
                for h in range(AH):
                    if h + 1 < AH:
                        scores(h + 1)
                    turn(h)
                    if h >= 1:
                        values(h - 1)
                values(AH - 1)
                pe.wait_ge(at_oq, AH * n + AH)
                for t in range(DT):
                    mm = nc.tensor.transpose(psf[:, t * P:(t + 1) * P], oq[:, t * P:(t + 1) * P], ident[:, :])
                mm.then_inc(at_ot, 1)

            pe.wait_ge(ck_out, 1)
            pe.wait_ge(kr_step, 16)
            blocks(pe, body)

        def act_attention(act):
            def body(n, kt):
                if isinstance(n, int):
                    act.wait_ge(qr_step, 3 * DT)
                else:
                    act.wait_ge(at_s, AH * n)
                nc.scalar.copy(q_st[:, :, :], proj[:, 0:DT, ds(n * P, P)]).then_inc(q_staged, 1)

                def exps(h):
                    u = AH * n + h
                    act.wait_ge(at_neg, u + 1)
                    after(act, at_t, u - 1)
                    o = 2 * (h % 2) * 512
                    nc.scalar.activation(pr[h % 2][:, 0:kt * P], psf[:, o:o + kt * P], ACT.Exp, bias=a_neg[:, h:h + 1],
                                         scale=ASCALE, accum_out=a_den[:, h:h + 1]).then_inc(at_p, 1)

                exps(0)
                for h in range(AH):
                    if h + 1 < AH:
                        exps(h + 1)
                    u = AH * n + h
                    act.wait_ge(at_t, u + 1)
                    after(act, at_o, u - 1)
                    w = min(4, kt) * P
                    nc.scalar.copy(pt[h % 2][:, 0:w], ps[:, 4, 0:w]).then_inc(at_ta, 1)
                act.wait_ge(at_ot, n + 1)
                nc.scalar.copy(h_hi[:, :, ds(n * P, P)], psf[:, 0:D].rearrange("p (t n) -> p t n", t=DT)).then_inc(at_hi, 1)

            blocks(act, body)

        def dve_attention(dve):
            def body(n, kt):
                def maxima(h):
                    u = AH * n + h
                    o = 2 * (h % 2) * 512
                    dve.wait_ge(at_s, u + 1)
                    after(dve, at_p, u - AH + 1)
                    nc.vector.reduce_max(a_max[:, h:h + 1], psf[:, o:o + kt * P], AX.X).then_inc(at_max, 1)
                    dve.wait_ge(at_max, u + 1)
                    nc.vector.tensor_scalar(a_neg[:, h:h + 1], a_max[:, h:h + 1], -ASCALE, None, ALU.mult).then_inc(at_neg, 1)

                def outputs(h):
                    u = AH * n + h
                    dve.wait_ge(at_p, u + 1)
                    nc.vector.reciprocal(a_rec[:, h:h + 1], a_den[:, h:h + 1]).then_inc(at_rec, 1)
                    dve.wait_ge(at_rec, u + 1)
                    dve.wait_ge(at_o, u + 1)
                    if h == 0:
                        after(dve, at_ot, n)
                    nc.vector.tensor_scalar(oq[:, h * HD:(h + 1) * HD], ps[:, 6 + h % 2, 0:HD], a_rec[:, h:h + 1], None,
                                            ALU.mult).then_inc(at_oq, 1)

                maxima(0)
                for h in range(AH):
                    if h + 1 < AH:
                        maxima(h + 1)
                    u = AH * n + h
                    dve.wait_ge(at_t, u + 1)
                    if kt == 5:
                        after(dve, at_o, u - 1)
                        nc.vector.tensor_copy(pt[h % 2][:, 4 * P:5 * P], ps[:, 5, 0:P]).then_inc(at_td, 1)
                    else:
                        dve.sem_inc(at_td, 1)
                    if h >= 1:
                        outputs(h - 1)
                outputs(AH - 1)
                dve.wait_ge(at_hi, n + 1)
                c = ds(n * P, P)
                nc.vector.tensor_tensor(h_lo[:, :, c], psf[:, 0:D].rearrange("p (t n) -> p t n", t=DT),
                                        h_hi[:, :, c].bitcast(F32), ALU.subtract).then_inc(at_lo, 1)

            blocks(dve, body)

        def act_odd(act):
            act_linear(act, "odd_in", 6)
            act_odd_prep(act)
            act_attention(act)
            act_linear(act, "odd_out", 4)
            act.wait_ge(kv_stored, 1)

        def dve_odd(dve):
            dve_odd_prep(dve)
            dve_attention(dve)
            dve_gate(dve, 4, 1, 1, 1.0, MOD_ALL)
            dve_add_groups(dve, "odd_out", 4, 4)

        def pe_odd(pe):
            pe_linear(pe, "odd_in", 6, (hlo_ready, 4 * DT))
            pe_odd_prep(pe)
            pe_attention(pe)
            pe.wait_ge(at_lo, TT)
            pe_linear(pe, "odd_out", 4, None)

        LAST_NORM = 6
        OUT_DMAS = 7
        y_tok = at("y_tok", [P, TT, D], o_h)

        def x_banks(t):
            o = (1 + 2 * (t % 3)) * 512
            return psf[:, o:o + T]

        def y_banks(t):
            o = 2 * (t % 2) * 512
            return psf[:, o:o + T].rearrange("p (b n) -> p b n", b=TT)

        def sp_store_y(sp):
            sp.wait_ge(y_out, DT)
            sp.dma_start(outs["y_prompt"][0], y_tok[:, 0, :]).then_inc(out_done, 16)
            sp.dma_start(outs["y_sample"][0].rearrange("(t p) d -> p t d", p=P), y_tok[:, 1:TT, :]).then_inc(out_done, 16)
            sp.wait_ge(out_done, 16 * OUT_DMAS)

        GATE_FREE = {1: GROUPS["even_in"], 2: GROUPS["ffn01"], 3: GROUPS["ffn10"], 4: GROUPS["odd_in"],
                     5: GROUPS["ffn11"]}

        block = ctx.enter_context(nc.Block())

        @block.sync
        def _(sp):
            sp.dma_start(rows[0:MT, 0, :], ins["mod_b"][0].rearrange("(a b) -> a b", b=P)).then_inc(rows_in, 16)
            sp.dma_start(rows[0:MT, 1, :], ins["mod_b"][1].rearrange("(a b) -> a b", b=P)).then_inc(rows_in, 16)
            for r0, src in ((ROWS["norm"], ins["norm_w"].rearrange("l j (a b) -> (l j a) b", b=P)),
                            (ROWS["final"], ins["final_norm_w"].rearrange("(a b) -> a b", b=P)),
                            (ROWS["cond"], ins["c_ctx"].rearrange("(a b) -> a b", b=P)),
                            (ROWS["cond"] + DT, ins["c"].rearrange("o (a b) -> (o a) b", b=P)),
                            (ROWS["conv"], ins["gdn_conv_w"].rearrange("e w (a b) -> (e w a) b", b=P))):
                sp.dma_start(rows[r0:r0 + src.shape[0], 2, :], src).then_inc(rows_in, 16)
            sp.dma_start(ident[:, :], ins["c_ident"]).then_inc(consts_in, 16)
            sp.dma_start(tri[:, :, :], ins["c_tri"]).then_inc(consts_in, 16)
            sp.dma_start(lvl_st[:, :, :, :], ins["c_lvl"]).then_inc(lvl_in, 16)
            mw0 = ins["mod_w"][0].rearrange("(k p) n -> p k n", p=P)
            for k in range(2):
                sp_mod_half(sp, k, 0, mw0, 0)
            sp.dma_start(x_tok[:, 0, :], ins["x_prompt"][0]).then_inc(x_in, 16)
            sp.dma_start(x_tok[:, 1:TT, :], ins["x_sample"][0].rearrange("(t p) d -> p t d", p=P)).then_inc(x_in, 16)
            for q in range(1, MOD_FIRST):
                for k in range(2):
                    sp_mod_half(sp, k, q, mw0, q)
            sp_mod_half(sp, 0, MOD_FIRST, mw0, MOD_FIRST)
            sp_ffn(sp, "ffn00")
            sp_even(sp)
            sp.wait_ge(mo_lo, 8)
            sp_ffn(sp, "ffn01")
            sp_ffn(sp, "ffn10")
            sp_odd(sp)
            sp_ffn(sp, "ffn11")
            sp_store_y(sp)

        @block.scalar
        def _(act):
            act.wait_ge(vecs_ready, 3)
            nc.scalar.activation(cond[:, :, :], vecs[:, ROWS["cond"]:ROWS["cond"] + 2 * DT].rearrange(
                "p (s k) -> p s k", s=2), ACT.Silu).then_inc(cond_ready, 1)
            for t in range(1, DT, 2):
                act.wait_ge(x_mm, t + 1)
                nc.scalar.copy(x[:, t, :], x_banks(t)).then_inc(x_act, 1)
            act.wait_ge(x_dve, DT // 2)
            act.wait_ge(x_act, DT // 2)
            for q in range(DT // 2):
                act_squares(act, 0, None, q)
            for g in range(2):
                act_split(act, g, g)
            act_ada(act, 0, 0, 0)
            act.wait_ge(lvl_ready, 1)
            act_ffn(act, "ffn00")
            act_ada(act, 1, 0, 1)
            act_even(act)
            act_ada(act, 2, 0, 2)
            act_ffn(act, "ffn01")
            act_ada(act, 3, 1, 0)
            act_ffn(act, "ffn10")
            act_ada(act, 4, 1, 1)
            act_odd(act)
            act_ada(act, 5, 1, 2)
            act_ffn(act, "ffn11")
            act_ada(act, LAST_NORM, 0, None)
            for t in range(DT):
                act.wait_ge(y_mm, t + 1)
                nc.scalar.copy(y_tok[:, :, t * P:(t + 1) * P], y_banks(t)).then_inc(y_out, 1)

        @block.vector
        def _(dve):
            nc.vector.memset(ones[:, :], 1.0).then_inc(consts_set, 1)
            nc.vector.memset(eps[:, :], EPS).then_inc(consts_set, 1)
            for r, (dst, n) in enumerate(((mod_b[:, 0:MT], MT), (mod_b[:, MT:2 * MT], MT), (vecs[:, :], NROWS))):
                dve.wait_ge(rows_mm, 3)
                nc.vector.tensor_copy(dst, ps[:, 0, r * P:r * P + n]).then_inc(vecs_ready, 1)
            for t in range(0, DT, 2):
                dve.wait_ge(x_mm, t + 1)
                nc.vector.tensor_copy(x[:, t, :], x_banks(t)).then_inc(x_dve, 1)
            dve.wait_ge(cond_ready, 1)
            dve.wait_ge(vecs_ready, 3)
            for q in range(MOD_FIRST):
                for k in range(2):
                    dve_mod_half(dve, k, q)
                dve_mod_out(dve, q, 0, q)
            dve_mod_half(dve, 0, MOD_FIRST)
            for g in range(2):
                dve_split(dve, g, g)
            dve_ada(dve, 0, 0, 0, MOD_FIRST)
            dve_ffn(dve, "ffn00", 0, 6)
            dve_ada(dve, 1, 0, 1, 12)
            dve_even(dve)
            dve_ada(dve, 2, 0, 2, 16)
            dve_ffn(dve, "ffn01", 2, 21)
            dve_ada(dve, 3, 1, 0, MOD_ALL)
            dve_ffn(dve, "ffn10", 3, MOD_ALL)
            dve_ada(dve, 4, 1, 1, MOD_ALL)
            dve_odd(dve)
            dve_ada(dve, 5, 1, 2, MOD_ALL)
            dve_ffn(dve, "ffn11", 5, MOD_ALL)
            dve_ada(dve, LAST_NORM, 0, None, 0)

        @block.tensor
        def _(pe):
            pe.wait_ge(rows_in, 16 * 7)
            pe.wait_ge(consts_in, 16 * 2)
            for r, n in enumerate((MT, MT, NROWS)):
                nc.tensor.transpose(ps[:, 0, r * P:r * P + n], rows[0:n, r, :], ident[0:n, 0:n]).then_inc(rows_mm, 1)
            pe.wait_ge(x_in, 32)
            pe.wait_ge(consts_set, 2)
            for t in range(DT):
                if t >= 3:
                    pe.wait_ge(x_dve if (t - 3) % 2 == 0 else x_act, (t - 3) // 2 + 1)
                for b in range(TT):
                    o = (1 + 2 * (t % 3)) * 512 + b * P
                    mm = nc.tensor.transpose(psf[:, o:o + P], x_tok[:, b, t * P:(t + 1) * P], ident[:, :])
                mm.then_inc(x_mm, 1)
            for q in range(MOD_FIRST):
                if q:
                    pe.wait_ge(mod_ready, q)
                pe_mod(pe, q)
            pe.wait_ge(mod_ready, MOD_FIRST)
            pe_ada(pe, 0)
            pe_ffn(pe, "ffn00", 0)
            pe_ada(pe, 1)
            pe_even(pe)
            pe_ada(pe, 2)
            pe_ffn(pe, "ffn01", 2)
            pe_ada(pe, 3)
            pe_ffn(pe, "ffn10", 3)
            pe_ada(pe, 4)
            pe_odd(pe)
            pe_ada(pe, 5)
            pe_ffn(pe, "ffn11", 5)
            pe_ada(pe, LAST_NORM)
            for t in range(DT):
                pe.wait_ge(hlo_ready, DT * LAST_NORM + t + 1)
                if t >= 2:
                    pe.wait_ge(y_out, t - 1)
                for b in range(TT):
                    o = 2 * (t % 2) * 512 + b * P
                    mm = nc.tensor.transpose(psf[:, o:o + P], TMP[t % 4][:, b * P:(b + 1) * P], ident[:, :])
                mm.then_inc(y_mm, 1)

        @block.gpsimd
        def _(pool):
            pool.wait_ge(lvl_in, 16)
            nc.gpsimd.tensor_copy(lvl[:, :, :, :], lvl_st[:, :, :, :]).then_inc(lvl_ready, 1)
            pool.wait_ge(lvl_ready, 1)
            pool.wait_ge(vecs_ready, 3)
            sums_cleared(pool, nc.gpsimd, 0)
            for q in range(DT // 2):
                add_squares(pool, nc.gpsimd, 0, q)
            pool_even(pool)


_INS = ['x_prompt', 'x_sample', 'state_ret', 'state_gdn', 'cache_k', 'cache_v', 'c', 'c_ctx', 'mod_w', 'mod_b', 'norm_w',
        'ffn_w_in', 'ffn_w_out', 'even_w_in', 'even_w_out', 'ret_decay_logit', 'ret_norm_w', 'gdn_conv_w', 'gdn_A_log',
        'gdn_dt_bias', 'gdn_norm_w', 'odd_w_in', 'odd_w_out', 'q_norm_w', 'k_norm_w', 'final_norm_w']
_OUTS = {'y_prompt': (1, NCTX, D), 'y_sample': (1, NLAT, D), 'new_state_ret': (1, 1, 2, RH, RDK, RDV),
         'new_state_gdn': (1, 1, 2, GH, GDK, 128), 'new_cache_k': (1, 1, NCTX, KVH, HD), 'new_cache_v': (1, 1, NCTX, KVH, HD)}


def shape_constants():
    import numpy as np
    r = np.arange(P)
    tri = (r[:, None] <= r[None, :]).astype(np.float32)
    lvl = np.zeros((P, 2, len(LEVELS), P), np.float32)
    for n, b in enumerate(LEVELS):
        same = (r[:, None] // (2 * b)) == (r[None, :] // (2 * b))
        m = same & (r[:, None] % (2 * b) < b) & (r[None, :] % (2 * b) >= b)
        lvl[:, 0, n] = m
        lvl[:, 1, n] = m.T
    dist = (np.arange(STRIP) - 384)[None, :] - r[:, None]
    pos = np.arange(NLAT)
    inv = 10000.0 ** (-np.arange(16, dtype=np.float32) / np.float32(16))
    inv = inv.astype(np.float32)
    ang = np.zeros((P, NLAT), np.float32)
    swap = np.zeros((P, P), np.float32)
    for p in range(P):
        d = p % HD
        part, e = d // 32, d % 32
        ang[p] = ((pos // 64) if part == 0 else (pos % 64)).astype(np.float32) * inv[e % 16]
        if e < 16:
            swap[p + 16, p] = -1.0
        else:
            swap[p - 16, p] = 1.0
    sel = np.zeros((P, 2, P), np.float32)
    for h in range(2):
        for m in range(P):
            sel[h * HD + m % HD, h, m] = 1.0
    half = np.zeros((P, 2), np.float32)
    half[:HD, 0] = 1.0
    half[HD:, 1] = 1.0
    return {
        'c_ident': np.eye(P, dtype=np.float32),
        'c_tri': np.ascontiguousarray(np.stack([tri, tri.T], axis=1)),
        'c_lvl': lvl,
        'c_dist': np.ascontiguousarray(np.stack([np.maximum(dist, 0), np.maximum(-dist, 0)], axis=1).astype(np.float32)),
        'c_pos': np.ascontiguousarray(np.broadcast_to(np.stack([pos + 1, NLAT - pos]).astype(np.float32), (P, 2, NLAT))),
        'c_rope': np.ascontiguousarray(np.stack([np.cos(ang), np.sin(ang)], axis=1).astype(np.float32)),
        'c_swap': swap,
        'c_sel': np.ascontiguousarray(np.concatenate([sel, np.stack([sel[:, h] @ swap for h in range(2)], axis=1)], axis=1)),
        'c_half': half,
    }


def kernel(**inputs):
    import numpy as np
    import concourse.bacc as bacc
    from concourse.bass_utils import run_bass_kernel_spmd as run

    nc = bacc.Bacc("TRN2", target_bir_lowering=False, num_devices=1)
    arrays = {name: np.ascontiguousarray(inputs[name]) for name in _INS}
    arrays.update(shape_constants())
    ins = {n: nc.dram_tensor(f"in_{n}_dram", a.shape, mybir.dt.from_np(a.dtype), kind="ExternalInput").ap()
           for n, a in arrays.items()}
    outs = {n: nc.dram_tensor(f"out_{n}_dram", s, F32, kind="ExternalOutput").ap() for n, s in _OUTS.items()}
    bass_hybrid_step(nc, ins, outs)
    r = run(nc, [{f"in_{n}_dram": a for n, a in arrays.items()}], core_ids=[0])
    return tuple(r.results[0][f"out_{n}_dram"] for n in _OUTS)
```
